# Optimizing a Trainium2 kernel written in Bass

```python
import math
import jax, jax.numpy as jnp
from jax import lax
import numpy as np
import jax
import jax.numpy as jnp

D_MODEL = 1024
BATCH = 1
SEQ = 512
DEPTH = 1

H_A = 8
DQK_A = D_MODEL // 16
DV_A = D_MODEL // 8
QK_A = H_A * DQK_A
V_A = H_A * DV_A
CHUNK = 64
CONV_K = 4
H_B = 8
HD_B = D_MODEL // 8
W_B = H_B * HD_B
QBLK = 128
D_FF = 4 * D_MODEL
EPS = 1e-6
IN_SIZES = (QK_A, QK_A, V_A, V_A, H_A, H_A, W_B, W_B, W_B, D_MODEL, D_MODEL)
IN_COLS = sum(IN_SIZES)


def rms_norm(x, g):
    xf = x.astype(jnp.float32)
    y = xf * lax.rsqrt(jnp.mean(xf * xf, axis=-1, keepdims=True) + EPS)
    return (y * g.astype(jnp.float32)).astype(x.dtype)

def head_rms_norm(x, g):
    xf = x.astype(jnp.float32)
    y = xf * lax.rsqrt(jnp.mean(xf * xf, axis=-1, keepdims=True) + EPS)
    return y * g.astype(jnp.float32)

def causal_conv(x, w):
    S = x.shape[1]
    xp = jnp.pad(x, ((0, 0), (CONV_K - 1, 0), (0, 0)))
    y = xp[:, 0:S] * w[0]
    for j in range(1, CONV_K):
        y = y + xp[:, j:j + S] * w[j]
    return y

def mlstm_chunkwise(q, k, v, i_pre, f_pre):
    B, S, H, _ = q.shape
    NC = S // CHUNK
    to_chunks = lambda a: jnp.moveaxis(a.astype(jnp.float32).reshape(B, NC, CHUNK, H, -1), 3, 1)
    q = to_chunks(q)
    k = to_chunks(k) * (DQK_A ** -0.5)
    v = to_chunks(v)
    gate = lambda a: jnp.moveaxis(a.astype(jnp.float32).reshape(B, NC, CHUNK, H), 3, 1)
    logf = jax.nn.log_sigmoid(gate(f_pre))
    ig = gate(i_pre)
    b = jnp.cumsum(logf, axis=-1)
    b_last = b[..., -1]

    a = b_last[..., None] - b + ig
    m_loc = jnp.max(a, axis=-1)
    w = jnp.exp(a - m_loc[..., None])
    S_loc = jnp.einsum('bhcs,bhcsk,bhcsv->bhckv', w, k, v)
    n_loc = jnp.einsum('bhcs,bhcsk->bhck', w, k)

    def step(carry, inp):
        S_prev, n_prev, m_prev = carry
        S_l, n_l, m_l, bl = inp
        m_new = jnp.maximum(bl + m_prev, m_l)
        sp = jnp.exp(bl + m_prev - m_new)
        sl = jnp.exp(m_l - m_new)
        S_new = sp[..., None, None] * S_prev + sl[..., None, None] * S_l
        n_new = sp[..., None] * n_prev + sl[..., None] * n_l
        return (S_new, n_new, m_new), (S_prev, n_prev, m_prev)

    init = (jnp.zeros_like(S_loc[:, :, 0]), jnp.zeros_like(n_loc[:, :, 0]), jnp.zeros_like(m_loc[:, :, 0]))
    xs = (jnp.moveaxis(S_loc, 2, 0), jnp.moveaxis(n_loc, 2, 0), jnp.moveaxis(m_loc, 2, 0), jnp.moveaxis(b_last, 2, 0))
    _, (S0, n0, m0) = lax.scan(step, init, xs)
    S0 = jnp.moveaxis(S0, 0, 2)
    n0 = jnp.moveaxis(n0, 0, 2)
    m0 = jnp.moveaxis(m0, 0, 2)

    causal = jnp.tril(jnp.ones((CHUNK, CHUNK), dtype=bool))
    D = jnp.where(causal, b[..., :, None] - b[..., None, :] + ig[..., None, :], -jnp.inf)
    b_inter = b + m0[..., None]
    m_t = jnp.maximum(b_inter, jnp.max(D, axis=-1))
    P = jnp.exp(D - m_t[..., None]) * jnp.einsum('bhctk,bhcsk->bhcts', q, k)
    inter = jnp.exp(b_inter - m_t)
    num = jnp.einsum('bhcts,bhcsv->bhctv', P, v) + inter[..., None] * jnp.einsum('bhctk,bhckv->bhctv', q, S0)
    den = jnp.sum(P, axis=-1) + inter * jnp.einsum('bhctk,bhck->bhct', q, n0)
    h = num / jnp.maximum(jnp.abs(den), jnp.exp(-m_t))[..., None]
    return jnp.moveaxis(h, 1, 3).reshape(B, S, H, DV_A)

def stick_breaking(q, k, v):
    S = q.shape[1]
    scale = HD_B ** -0.5
    outs = []
    for blk in range(S // QBLK):
        t0, t1 = blk * QBLK, (blk + 1) * QBLK
        z = jnp.einsum('bqhd,bshd->bhqs', q[:, t0:t1], k[:, :t1]) * scale
        t_idx = t0 + jnp.arange(QBLK)
        s_idx = jnp.arange(t1)
        strict = s_idx[None, :] < t_idx[:, None]
        log_keep = jnp.where(strict, jax.nn.log_sigmoid(-z), 0.0)
        suffix = lax.cumsum(log_keep, axis=3, reverse=True) - log_keep
        A = jnp.where(strict, jnp.exp(jax.nn.log_sigmoid(z) + suffix), 0.0)
        outs.append(jnp.einsum('bhqs,bshd->bqhd', A, v[:, :t1]))
    return jnp.concatenate(outs, axis=1)

def first_inputs(seed: int = 0) -> dict:
    key = jax.random.key(seed)
    ks = jax.random.split(key, 15)
    n = jax.random.normal
    f32 = jnp.float32
    x = n(ks[0], (BATCH, SEQ, D_MODEL), f32)
    norm_mix_g = 1.0 + 0.1 * n(ks[1], (DEPTH, D_MODEL), f32)
    w_in = n(ks[2], (DEPTH, D_MODEL, IN_COLS), f32) * D_MODEL ** -0.5
    b_if = jnp.concatenate([0.5 * n(ks[3], (DEPTH, H_A), f32),
                            3.0 + 0.5 * n(ks[4], (DEPTH, H_A), f32)], axis=-1)
    b_gate = 0.02 * n(ks[5], (DEPTH, 2 * D_MODEL), f32)
    conv_w = n(ks[6], (DEPTH, CONV_K, 2 * QK_A), f32) * CONV_K ** -0.5
    mlstm_norm_g = 1.0 + 0.1 * n(ks[7], (DEPTH, V_A), f32)
    sb_q_norm_g = 1.0 + 0.1 * n(ks[8], (DEPTH, HD_B), f32)
    sb_k_norm_g = 1.0 + 0.1 * n(ks[9], (DEPTH, HD_B), f32)
    w_out = n(ks[10], (DEPTH, D_MODEL, D_MODEL), f32) * D_MODEL ** -0.5
    norm_mlp_g = 1.0 + 0.1 * n(ks[11], (DEPTH, D_MODEL), f32)
    w_up = n(ks[12], (DEPTH, D_MODEL, D_FF), f32) * D_MODEL ** -0.5
    w_down = n(ks[13], (DEPTH, D_FF, D_MODEL), f32) * D_FF ** -0.5
    return {"x": x, "norm_mix_g": norm_mix_g, "w_in": w_in, "b_if": b_if, "b_gate": b_gate,
            "conv_w": conv_w, "mlstm_norm_g": mlstm_norm_g, "sb_q_norm_g": sb_q_norm_g,
            "sb_k_norm_g": sb_k_norm_g, "w_out": w_out, "norm_mlp_g": norm_mlp_g,
            "w_up": w_up, "w_down": w_down}

def first_block(x, norm_mix_g, w_in, b_if, b_gate, conv_w, mlstm_norm_g, sb_q_norm_g, sb_k_norm_g,
              w_out, norm_mlp_g, w_up, w_down):
    B, S, _ = x.shape
    split_idx = np.cumsum(IN_SIZES)[:-1].tolist()
    for l in range(DEPTH):
        h = rms_norm(x, norm_mix_g[l])
        p = h @ w_in[l]
        q_a, k_a, v_a, o_a, i_a, f_a, q_b, k_b, v_b, g_a, g_b = jnp.split(p, split_idx, axis=-1)
        qk_a = jax.nn.silu(causal_conv(jnp.concatenate([q_a, k_a], axis=-1), conv_w[l]))
        q_a, k_a = qk_a[..., :QK_A], qk_a[..., QK_A:]
        i_pre = i_a.astype(jnp.float32) + b_if[l, :H_A].astype(jnp.float32)
        f_pre = f_a.astype(jnp.float32) + b_if[l, H_A:].astype(jnp.float32)
        h_a = mlstm_chunkwise(q_a.reshape(B, S, H_A, DQK_A), k_a.reshape(B, S, H_A, DQK_A),
                              v_a.reshape(B, S, H_A, DV_A), i_pre, f_pre)
        h_a = head_rms_norm(h_a, mlstm_norm_g[l].reshape(H_A, DV_A)).reshape(B, S, V_A)
        y_a = jax.nn.sigmoid(o_a.astype(jnp.float32)) * h_a
        qn = head_rms_norm(q_b.reshape(B, S, H_B, HD_B), sb_q_norm_g[l])
        kn = head_rms_norm(k_b.reshape(B, S, H_B, HD_B), sb_k_norm_g[l])
        y_b = stick_breaking(qn, kn, v_b.reshape(B, S, H_B, HD_B).astype(jnp.float32)).reshape(B, S, W_B)
        gates = jax.nn.sigmoid(jnp.concatenate([g_a, g_b], axis=-1).astype(jnp.float32)
                               + b_gate[l].astype(jnp.float32))
        y = gates[..., :D_MODEL] * y_a + gates[..., D_MODEL:] * y_b
        x = x + y.astype(x.dtype) @ w_out[l]
        h2 = rms_norm(x, norm_mlp_g[l])
        x = x + jnp.square(jax.nn.relu(h2 @ w_up[l])) @ w_down[l]
    return x


DEPTH_2 = 2

EXPAND = 2
MIX_WIDTH = EXPAND * D_MODEL
HG_WIDTH = MIX_WIDTH // 2
HG_HEAD_DIM = 128
HG_HEADS = HG_WIDTH // HG_HEAD_DIM
HG_CHUNK = 64
ATT_WIDTH = MIX_WIDTH - HG_WIDTH
ATT_HEAD_DIM = 64
ATT_HEADS = ATT_WIDTH // ATT_HEAD_DIM
ATT_KV_HEADS = max(1, ATT_HEADS // 8)
ATT_GROUP = ATT_HEADS // ATT_KV_HEADS
KV_WIDTH = ATT_KV_HEADS * ATT_HEAD_DIM
WINDOW = 128
ATT_BLOCK = 128
ATT_SCALE = 1.0 / math.sqrt(ATT_HEAD_DIM)
ROPE_THETA = 10000.0
NORM_EPS = 1e-6
NEG_INF = -1e30
LB_FLOOR = 1e-20

SPLIT_SIZES = (HG_WIDTH, HG_WIDTH, HG_WIDTH, HG_WIDTH, ATT_WIDTH, KV_WIDTH, KV_WIDTH, ATT_WIDTH)
IN_WIDTH = int(sum(SPLIT_SIZES))
SPLIT_POINTS = tuple(int(v) for v in np.cumsum(SPLIT_SIZES)[:-1])


def rms_norm_2(x, g):
    xf = x.astype(jnp.float32)
    y = xf * lax.rsqrt(jnp.mean(xf * xf, axis=-1, keepdims=True) + NORM_EPS)
    return (y * g.astype(jnp.float32)).astype(x.dtype)

def rotary(x, pos):
    half = x.shape[-1] // 2
    inv_freq = ROPE_THETA ** (-jnp.arange(half, dtype=jnp.float32) / half)
    ang = pos.astype(jnp.float32)[:, None] * inv_freq[None, :]
    cos = jnp.cos(ang)[None, :, None, :]
    sin = jnp.sin(ang)[None, :, None, :]
    xf = x.astype(jnp.float32)
    x1, x2 = xf[..., :half], xf[..., half:]
    return jnp.concatenate([x1 * cos - x2 * sin, x2 * cos + x1 * sin], axis=-1).astype(x.dtype)

def hgrn2(q, f_logit, i, lb):
    B, S, _ = q.shape
    C, H, D = HG_CHUNK, HG_HEADS, HG_HEAD_DIM
    nC = S // C
    lb = lb.astype(jnp.float32)
    qf = jax.nn.silu(q.astype(jnp.float32))
    logf = jnp.logaddexp(jnp.log(jnp.maximum(lb, LB_FLOOR)),
                         jnp.log1p(-lb) + jax.nn.log_sigmoid(f_logit.astype(jnp.float32)))
    k = -jnp.expm1(logf)

    def chunks(t):
        return t.reshape(B, nC, C, H, D).transpose(1, 0, 3, 2, 4)

    qc, kc, vc, gc = chunks(qf), chunks(k), chunks(i.astype(jnp.float32)), chunks(logf)
    bc = jnp.cumsum(gc, axis=3)
    causal = jnp.tril(jnp.ones((C, C), dtype=bool))[None, None, :, :, None]

    def step(state, xs):
        qch, kch, vch, b = xs
        b_last = b[:, :, C - 1:C, :]
        diff = b[:, :, :, None, :] - b[:, :, None, :, :]
        decay = jnp.where(causal, jnp.exp(jnp.where(causal, diff, 0.0)), 0.0)
        scores = jnp.einsum('bhtd,bhsd,bhtsd->bhts', qch, kch, decay)
        o = jnp.einsum('bhts,bhsv->bhtv', scores, vch)
        o = o + jnp.einsum('bhtd,bhdv->bhtv', qch * jnp.exp(b), state)
        state = jnp.exp(b_last[:, :, 0, :])[..., None] * state + \
            jnp.einsum('bhsd,bhsv->bhdv', kch * jnp.exp(b_last - b), vch)
        return state, o

    s0 = jnp.zeros((B, H, D, D), dtype=jnp.float32)
    _, o = lax.scan(step, s0, (qc, kc, vc, bc))
    return o.transpose(1, 0, 3, 2, 4).reshape(B, S, H, D)

def sliding_window_attention(q, k, v, sinks):
    B, S = q.shape[0], q.shape[1]
    L, KV, G, D = ATT_BLOCK, ATT_KV_HEADS, ATT_GROUP, ATT_HEAD_DIM
    nB = S // L
    qb = q.reshape(B, nB, L, KV, G, D)
    kb = k.reshape(B, nB, L, KV, D)
    vb = v.reshape(B, nB, L, KV, D)
    k_prev = jnp.concatenate([jnp.zeros_like(kb[:, :1]), kb[:, :-1]], axis=1)
    v_prev = jnp.concatenate([jnp.zeros_like(vb[:, :1]), vb[:, :-1]], axis=1)
    kw = jnp.concatenate([k_prev, kb], axis=2)
    vw = jnp.concatenate([v_prev, vb], axis=2)
    s = jnp.einsum('bnqkgd,bnskd->bnkgqs', qb, kw).astype(jnp.float32) * ATT_SCALE
    qpos = jnp.arange(L)[:, None] + L
    kpos = jnp.arange(2 * L)[None, :]
    diff = qpos - kpos
    band = (diff >= 0) & (diff < WINDOW)
    key_exists = (jnp.arange(nB)[:, None] * L - L + jnp.arange(2 * L)[None, :]) >= 0
    mask = band[None, :, :] & key_exists[:, None, :]
    s = jnp.where(mask[None, :, None, None, :, :], s, NEG_INF)
    sink = jnp.broadcast_to(sinks.astype(jnp.float32).reshape(KV, G)[None, None, :, :, None, None],
                            s.shape[:-1] + (1,))
    p = jax.nn.softmax(jnp.concatenate([s, sink], axis=-1), axis=-1)[..., :-1]
    o = jnp.einsum('bnkgqs,bnskd->bnqkgd', p.astype(v.dtype), vw)
    return o.reshape(B, S, KV * G * D)

def hybrid_layer(x, w_in, w_out, g_pre, g_post, lb, g_head, sinks):
    B, S, _ = x.shape
    h = rms_norm_2(x, g_pre)
    proj = jnp.einsum('bsd,de->bse', h, w_in)
    q_h, f_h, i_h, z_h, q_a, k_a, v_a, z_a = jnp.split(proj, SPLIT_POINTS, axis=-1)

    o_h = hgrn2(q_h, f_h, i_h, lb)
    o_h = rms_norm_2(o_h, g_head).reshape(B, S, HG_WIDTH).astype(z_h.dtype) * jax.nn.silu(z_h)

    pos = jnp.arange(S)
    q_a = rotary(q_a.reshape(B, S, ATT_HEADS, ATT_HEAD_DIM), pos)
    k_a = rotary(k_a.reshape(B, S, ATT_KV_HEADS, ATT_HEAD_DIM), pos)
    v_a = v_a.reshape(B, S, ATT_KV_HEADS, ATT_HEAD_DIM)
    o_a = sliding_window_attention(q_a, k_a, v_a, sinks).astype(z_a.dtype) * jax.nn.silu(z_a)

    y = jnp.einsum('bse,ed->bsd', jnp.concatenate([o_h, o_a], axis=-1), w_out)
    return x + rms_norm_2(y, g_post)

def second_inputs(seed: int = 0) -> dict:
    key = jax.random.key(seed)
    ks = jax.random.split(key, 9)
    x = jax.random.normal(ks[0], (BATCH, SEQ, D_MODEL), dtype=jnp.float32)
    w_in = jax.random.normal(ks[1], (DEPTH_2, D_MODEL, IN_WIDTH), dtype=jnp.float32) * D_MODEL ** -0.5
    w_out = jax.random.normal(ks[2], (DEPTH_2, MIX_WIDTH, D_MODEL), dtype=jnp.float32) * MIX_WIDTH ** -0.5
    g_pre = 1.0 + 0.05 * jax.random.normal(ks[3], (DEPTH_2, D_MODEL), dtype=jnp.float32)
    g_post = 1.0 + 0.05 * jax.random.normal(ks[4], (DEPTH_2, D_MODEL), dtype=jnp.float32)
    lb_param = 0.1 * jax.random.normal(ks[5], (DEPTH_2, HG_WIDTH), dtype=jnp.float32)
    g_head = 1.0 + 0.05 * jax.random.normal(ks[6], (DEPTH_2, HG_HEAD_DIM), dtype=jnp.float32)
    sinks = jax.random.normal(ks[7], (DEPTH_2, ATT_HEADS), dtype=jnp.float32)
    return {"x": x, "w_in": w_in, "w_out": w_out, "g_pre": g_pre, "g_post": g_post,
            "lb_param": lb_param, "g_head": g_head, "sinks": sinks}

def second_block(x, w_in, w_out, g_pre, g_post, lb_param, g_head, sinks):
    p = jax.nn.softmax(lb_param.astype(jnp.float32), axis=0)
    lower_bounds = jnp.cumsum(p, axis=0) - p[0:1]
    for l in range(DEPTH_2):
        x = hybrid_layer(x, w_in[l], w_out[l], g_pre[l], g_post[l], lower_bounds[l], g_head[l], sinks[l])
    return x


def setup_inputs(seed=0):
    out = dict(first_inputs(seed))
    for name, value in second_inputs(seed + 1).items():
        if name != "x":
            out[name + "_2"] = value
    return out


def reference(
    x, norm_mix_g, w_in, b_if, b_gate, conv_w, mlstm_norm_g, sb_q_norm_g, sb_k_norm_g, w_out,
    norm_mlp_g, w_up, w_down, w_in_2, w_out_2, g_pre_2, g_post_2, lb_param_2, g_head_2, sinks_2,
):
    x = first_block(
        x, norm_mix_g, w_in, b_if, b_gate, conv_w, mlstm_norm_g, sb_q_norm_g, sb_k_norm_g,
        w_out, norm_mlp_g, w_up, w_down,
    )
    return second_block(
        x, w_in_2, w_out_2, g_pre_2, g_post_2, lb_param_2, g_head_2, sinks_2,
    )


_drawn_inputs = setup_inputs


def setup_inputs(seed=0):
    import zlib

    import numpy as np

    out = dict(_drawn_inputs(seed))
    spreads = {}
    factors = {'b_gate': 8.0, 'sb_q_norm_g': 2.842, 'lb_param_2': 8.0, 'sinks_2': 6.536}
    for name, (base, spread) in spreads.items():
        noise = np.random.default_rng([zlib.crc32(name.encode()), seed]).standard_normal(out[name].shape)
        drawn = base * np.exp(spread * noise) if base else spread * noise
        out[name] = jnp.asarray(drawn.astype(out[name].dtype))
    for name, factor in factors.items():
        out[name] = (out[name] * factor).astype(out[name].dtype)
    return out
```

```python
from contextlib import ExitStack

import numpy as np

import concourse.bass as bass
from concourse import mybir
from concourse.alu_op_type import AluOpType as ALU

F32 = mybir.dt.float32
F32R = mybir.dt.float32r
BF16 = mybir.dt.bfloat16
U32 = mybir.dt.uint32
ACT = mybir.ActivationFunctionType
AX = mybir.AxisListType

P = 128
S = 512
NT = S // P
DM = 1024
KT = DM // P
EPS = 1e-6
NEG = -1e30

C_QA, C_KA, C_VA, C_OA, C_IF = 0, 512, 1024, 2048, 3072
C_QB, C_KB, C_VB, C_GA, C_GB = 3088, 4112, 5136, 6160, 7184
C_HQ, C_HF, C_HI, C_HZ, C_AQ, C_AK, C_AV, C_AZ = 0, 1024, 2048, 3072, 4096, 5120, 5248, 5376

R_NMIX, R_BGATE, R_CONV, R_MG, R_SBQ, R_SBK, R_NMLP = 0, 8, 24, 56, 64, 65, 66
R_GPRE, R_GPOST, R_LB, R_GHEAD, R_END = 74, 90, 106, 122, 124

REG = [0, 512, 1024, 896]
REGLEN = [S - P * i for i in range(NT)]
ZPART = [slice(0, 512), slice(512, 1280)]
OFF = [0, 512, 384]

K_ID, K_ONES, K_NEGONES, K_TRI, K_NEGTRI, K_SNEG, K_CNEG, K_STRICT, K_ROT = [P * i for i in range(9)]
K_LEVEL = 9 * P
K_WIN = K_LEVEL + 7 * 64
K_COS = K_WIN + 512
K_SIN = K_COS + S
K_END = K_SIN + S

def ln_pair():
    s = np.arange(np.float32(7.0).view(np.uint32), np.float32(7.0).view(np.uint32) + 400000, dtype=np.uint32).view(np.float32)
    ln = np.log(s.astype(np.float64))
    i = int(np.argmin(np.abs(ln - ln.astype(np.float32))))
    return float(s[i]), float(np.float32(ln[i]))


def constants():
    c = np.zeros((P, K_END), np.float32)
    i, j = np.arange(P)[:, None], np.arange(P)[None, :]
    c[:, K_ID:K_ID + P] = i == j
    c[:, K_ONES:K_ONES + P] = 1
    c[:, K_NEGONES:K_NEGONES + P] = -1
    c[:, K_TRI:K_TRI + P] = i <= j
    c[:, K_NEGTRI:K_NEGTRI + P] = -1.0 * (i >= j)
    c[:, K_SNEG:K_SNEG + P] = np.where(i < j, 0, NEG)
    c[:, K_CNEG:K_CNEG + P] = np.where(i <= j, 0, NEG)
    c[:, K_STRICT:K_STRICT + P] = i < j
    d = j % 64
    c[:, K_ROT:K_ROT + P] = np.where((d < 32) & (i == j + 32), -1, 0) + np.where((d >= 32) & (i == j - 32), 1, 0)
    for n in range(7):
        L = 64 >> n
        t = np.arange(64)
        t = (t // L) * 2 * L + L + t % L
        s = np.arange(P)[:, None]
        c[:, K_LEVEL + 64 * n:K_LEVEL + 64 * n + 64] = (s // (2 * L) == t // (2 * L)) & (s % (2 * L) < L)
    q, k = i + P, np.arange(2 * P)[None, :]
    band = (q - k >= 0) & (q - k < P)
    c[:, K_WIN:K_WIN + 256] = np.where(band & (k >= P), 0, NEG)
    c[:, K_WIN + 256:K_WIN + 512] = np.where(band, 0, NEG)
    half = 32
    inv = (np.float32(10000.0) ** (-np.arange(half, dtype=np.float32) / np.float32(half))).astype(np.float32)
    ang = np.arange(S, dtype=np.float32)[None, :] * inv[np.arange(P) % half][:, None]
    c[:, K_COS:K_COS + S] = np.cos(ang)
    c[:, K_SIN:K_SIN + S] = np.sin(ang)
    return c


def build(nc, t, out):
    ctx = ExitStack()
    LNS, LNC = ln_pair()

    def sb(name, shape, dt=F32):
        return ctx.enter_context(nc.sbuf_tensor(name, shape, dt))

    def sem(name):
        return ctx.enter_context(nc.semaphore(name))

    x = sb("x", [P, KT, S])
    h1 = sb("h1", [P, KT, S], F32R)
    h2 = sb("h2", [P, KT, S], F32R)
    y = sb("y", [P, 2 * KT, S])
    ring = ExitStack()
    w_raw = ring.enter_context(nc.sbuf_tensor("w_raw", [P, 4, DM], F32))
    ring.close()
    w2 = sb("w2", [P, 4, DM], F32R)
    w1 = sb("w1", [P, 4, DM], F32R)
    cst = sb("cst", [P, K_LEVEL])
    par = sb("par", [P, P])
    epsc = sb("epsc", [P, 1])
    tick = sb("tick", [P, 4])
    ptick = sb("ptick", [P, 1])
    nsq = sb("nsq", [P, 2, S])
    nhf = sb("nhf", [P, 2, S])
    rstd = sb("rstd", [P, S])
    xin = y[:, 0:KT, :].rearrange("p (n a) s -> p n (a s)", n=NT)
    xout = y[:, KT:2 * KT, :].rearrange("p (n a) s -> p n (a s)", n=NT)
    squares = y[:, KT:2 * KT, :]
    ps = ctx.enter_context(nc.psum_tensor("ps", [P, 8, S], F32))
    G = [ps[:, 0, :], ps[:, 1, :]]
    M = [ps[:, 2 + i, :] for i in range(6)]
    FZ = ps[:, 2:5, :].rearrange("p b n -> p (b n)")

    ident = cst[:, K_ID:K_ID + P]
    ones = cst[:, K_ONES:K_ONES + P]

    one = ExitStack()

    def sb1(name, shape, dt=F32):
        return one.enter_context(nc.sbuf_tensor(name, shape, dt))

    rows = sb1("rows", [P, P])
    wif = sb1("wif", [P, KT, 16])
    wif1 = sb1("wif1", [P, KT, 16], F32R)
    wif2 = sb1("wif2", [P, KT, 16], F32R)
    bif = sb1("bif", [1, 16])
    ifs = sb1("ifs", [P, NT, 16])
    gt = sb1("gt", [P, NT, 8])
    logf = sb1("logf", [P, NT, 8])
    b_tok = sb1("b_tok", [P, NT, 8])
    c_tok = sb1("c_tok", [P, NT, 8])
    c_row = sb1("c_row", [8, S])
    m_row = sb1("m_row", [8, S])
    e_row = sb1("e_row", [8, S])
    qb, kb, vb, va, oa, ga, gb = ([sb1(f"{n}{i}", [P, S]) for i in range(2)] for n in ("qb", "kb", "vb", "va", "oa", "ga", "gb"))
    negm, ebc = ([sb1(f"{n}{i}", [P, S]) for i in range(2)] for n in ("negm", "ebc"))
    curp = [sb1(f"curp{i}", [P, 8]) for i in range(2)]
    convp = sb1("convp", [P, 8])
    qpad, kpad = sb1("qpad", [P, S + 8]), sb1("kpad", [P, S + 8])
    qa, ka = sb1("qa", [P, S]), sb1("ka", [P, S])
    lbuf = sb1("lbuf", [P, 1280])
    wbuf = sb1("wbuf", [P, 1280])
    sq = sb1("sq", [P, 2, S])
    t0, t1, t2, t3 = (sb1(f"t{i}", [P, S]) for i in range(4))

    one.close()
    mlp = ExitStack()
    a1 = mlp.enter_context(nc.sbuf_tensor("a1", [P, KT, S], F32R))
    a2 = mlp.enter_context(nc.sbuf_tensor("a2", [P, KT, S], F32R))
    hid = mlp.enter_context(nc.sbuf_tensor("hid", [P, 2, S], F32))
    mlp.close()

    two = ExitStack()

    def sb2(name, shape, dt=F32):
        return two.enter_context(nc.sbuf_tensor(name, shape, dt))

    hq, hf, hv, hz, aq, az = ([sb2(f"{n}{i}", [P, S]) for i in range(2)] for n in ("hq", "hf", "hv", "hz", "aq", "az"))
    bb, kk = sb2("bb", [P, S]), sb2("kk", [P, S])
    lev = sb2("lev", [P, 3, S])
    kt, qt = sb2("kt", [P, 2, S]), sb2("qt", [P, 2, 256])
    qe, xe, kg = sb2("qe", [P, 384]), sb2("xe", [P, 384]), sb2("kg", [P, 384])
    etot = sb2("etot", [P, 4])
    p_off, p_diag = sb2("p_off", [P, 768]), sb2("p_diag", [P, S])
    prob = sb2("prob", [P, 2, 1024])
    arot = sb2("arot", [P, S])
    kd = [sb2(f"kd{i}", [P, S]) for i in range(2)]
    av = sb2("av", [P, S])
    cosin = sb2("cosin", [P, 2, S])
    lmask = sb2("lmask", [P, 7, 256], mybir.dt.uint8)
    wmask = sb2("wmask", [P, 2, 256], BF16)
    identb = sb2("identb", [P, P], BF16)
    lnc = sb2("lnc", [P, P])
    lbp = sb2("lbp", [P, 2, 4, 8])
    lbt = sb2("lbt", [P, 6, 8])
    sinkb = sb2("sinkb", [P, 32])
    curh = [sb2(f"curh{i}", [P, 8]) for i in range(2)]
    sm = sb2("sm", [P, 6, 8])
    two.close()
    T = [nsq[:, 0, :], nsq[:, 1, :], nhf[:, 0, :], nhf[:, 1, :], rstd[:, :]]

    scr_m = nc.dram_tensor("scr_m", [8, S], F32).ap()
    scr_e = nc.dram_tensor("scr_e", [8, S], F32).ap()

    s_rows, s_cst, s_out = sem("rows_loaded"), sem("cst_loaded"), sem("out_stored")
    s_scr = sem("scratch_stored")
    raw = [sem(f"unit_loaded{i}") for i in range(4)]
    w_hi, w_lo, unit, evac = sem("w_hi_made"), sem("w_split"), sem("unit_multiplied"), sem("unit_evacuated")
    a_ser, d_ser, p_ser = sem("act_step"), sem("dve_step"), sem("pool_step")
    E = {}

    def ev(name):
        if name not in E:
            E[name] = sem(name)
        return E[name]

    def norm_bank(n):
        return G[0] if n == 1 else M[5]

    def norm_lo(n, k):
        return ev(("norm_lo_even", "norm_lo_odd")[k % 2]), n * 4 + k // 2 + 1

    def x_added(l, k):
        return (ev("x_added_even"), 4 * l + k // 2 + 1) if k % 2 == 0 else (ev("x_added"), 8 + 4 * l + k // 2 + 1)

    def evac_of(u, l):
        return u + (64 - u_two + 1 - (per_layer - 50) * l)

    def att_tile(j, b):
        return j + KT if b == 1 else j + (KT + 3)

    class Serial:

        def __init__(self, eng, s):
            self.eng, self.s, self.base, self.n = eng, s, 0, 0

        def at(self, base, s=None):
            self.base, self.n = base, 0
            if s is not None:
                self.s = s

        def __call__(self, ins):
            ins.then_inc(self.s, 1)
            self.n += 1
            self.eng.wait_ge(self.s, self.base + self.n)

        def flag(self, ins, name, value):
            ins.then_inc(ev(name), 1)
            self.eng.wait_ge(ev(name), value)

    u_out = 64
    u_mlp = 72
    u_two = 136
    per_layer = 66

    block = ctx.enter_context(nc.Block())

    def diag(buf, n):
        if n == 0:
            return buf[:, 0:1024].rearrange("p (n w) -> p n w", w=S)[:, :, 0:P]
        return buf[:, REG[3]:REG[3] + 2 * P].rearrange("p (n w) -> p n w", w=P)

    def mask2(c):
        return cst[:, c:c + P].unsqueeze(1).broadcast_to([P, 2, P])

    def w_unit(j, i):
        w = t["w_in"][0].rearrange("(k p) n -> p k n", p=P)
        per = [(C_QB, 1), (C_KB, 1), (C_VB, 1), (C_VA, 1), (C_OA, 1), (C_GA, 1), (C_GB, 1)]
        if i < 7:
            c = per[i][0] + j * 256
        elif i == 7:
            c = C_QA + j * 128
        elif i == 8:
            c = C_KA + j * 128
        else:
            c = per[i - 9][0] + P + j * 256
        return w[:, :, bass.ds(c, P)]

    @block.sync
    def _(sp):
        cols = lambda slot: w_raw[:, slot, :].rearrange("p (k n) -> p k n", k=KT)

        for n in range(NT):
            sp.dma_start(xin[:, n, :], t["x"][0, P * n:P * n + P, :]).then_inc(ev(f"x_loaded{n}"), 16)
        sp.dma_start(cst[:, :], t["consts"][:, 0:K_LEVEL]).then_inc(s_cst, 16)
        sp.dma_start(wif[:, :, :], t["w_in"][0].rearrange("(k p) n -> p k n", p=P)[:, :, C_IF:C_IF + 16]).then_inc(s_cst, 16)
        sp.dma_start(bif[:, :], t["b_if"]).then_inc(s_cst, 16)
        for r, n, a in ((R_NMIX, 8, t["norm_mix_g"]), (R_BGATE, 16, t["b_gate"]), (R_MG, 8, t["mlstm_norm_g"]),
                        (R_SBQ, 1, t["sb_q_norm_g"]), (R_SBK, 1, t["sb_k_norm_g"]), (R_NMLP, 8, t["norm_mlp_g"]),
                        (R_GPRE, 16, t["g_pre_2"]), (R_GPOST, 16, t["g_post_2"]), (R_LB, 16, t["lb_param_2"]),
                        (R_GHEAD, 2, t["g_head_2"])):
            sp.dma_start(rows[r:r + n, :], a.rearrange("l (r n) -> (l r) n", n=P)).then_inc(s_rows, 16)
        sp.dma_start(rows[R_CONV:R_CONV + 32, :], t["conv_w"][0].rearrange("c (r n) -> (c r) n", n=P)).then_inc(s_rows, 16)
        for i in range(4):
            sp.dma_start(cols(i), w_unit(0, i)).then_inc(raw[i], 16)
        with nc.sync.Fori(0, 3) as j:
            for i in range(4, 20):
                sp.wait_ge(unit, j * 16 + i - 3)
                sp.dma_start(cols(i % 4), w_unit(j + i // 16, i % 16)).then_inc(raw[i % 4], 16)
        for i in range(4, 16):
            sp.wait_ge(unit, 48 + i - 3)
            sp.dma_start(cols(i % 4), w_unit(3, i)).then_inc(raw[i % 4], 16)
        for k in range(KT):
            sp.wait_ge(unit, u_out + k - 3)
            sp.dma_start(w_raw[:, k % 4, :], t["w_out"][0][P * k:P * k + P, :]).then_inc(raw[k % 4], 16)
        sp.wait_ge(ev("mix_done"), 9)
        sp.dma_start(cosin[:, :, :], t["consts"][:, K_COS:K_END].rearrange("p (a n) -> p a n", a=2)).then_inc(ev("consts2"), 16)
        sp.dma_start(prob[:, 0, 0:960], t["consts"][:, K_LEVEL:K_COS]).then_inc(ev("consts2"), 16)
        sp.dma_start(sinkb[:, :], t["sinks_2"].rearrange("l h -> (l h)").unsqueeze(0).broadcast_to([P, 32])).then_inc(ev("consts2"), 16)

        with nc.sync.Fori(0, 4) as c:
            for i in range(16):
                sp.wait_ge(unit, c * 16 + (u_mlp + i - 3))
                if i < 8:
                    src = t["w_up"][0].rearrange("(k p) n -> p k n", p=P)[:, :, bass.ds(c * DM + P * i, P)]
                else:
                    src = t["w_down"][0].rearrange("(c k p) n -> c p k n", p=P, k=KT)[bass.ds(c, 1), :, :, P * (i - 8):P * (i - 7)]
                    src = src.rearrange("c p k n -> (c p) k n")
                sp.dma_start(cols(i % 4), src).then_inc(raw[i % 4], 16)
        def load2(off, q, src):
            u = u_two + off
            sp.wait_ge(unit, q * 4 + (u - 3))
            s_ = u % 4
            dst = w_raw[:, s_, :]
            if len(src.shape) == 3:
                dst = dst.rearrange("p (k n) -> p k n", k=KT)
            sp.dma_start(dst, src).then_inc(raw[s_], 16)

        for l in range(2):
            wl = t["w_in_2"][l].rearrange("(k p) n -> p k n", p=P)
            o = per_layer * l
            load2(o, 0, wl[:, :, C_AK:C_AK + P])
            load2(o + 1, 0, wl[:, :, C_AV:C_AV + P])
            with nc.sync.Fori(0, 4) as j:
                for b in range(2):
                    for i, (c, st, tile) in enumerate(((C_HQ, 256, 1), (C_HF, 256, 1), (C_HI, 256, 1), (C_HZ, 256, 1),
                                                       (C_AQ, 128, 4), (C_AZ, 128, 4))):
                        load2(o + 2 + 6 * b + i, j * 3, wl[:, :, bass.ds(j * st + (c + P * tile * b), P)])
            for k in range(2 * KT):
                load2(o + 50 + k, 0, t["w_out_2"][l][P * k:P * k + P, :])
        for half_ in range(2):
            c = slice(512 * half_, 512 * half_ + 512)
            sp.wait_ge(ev("out_rows"), 4 * half_ + 4)
            sp.dma_start(out[0].rearrange("(n p) d -> p n d", p=P)[:, :, c], xout[:, :, c]).then_inc(s_out, 16)
        sp.wait_ge(s_out, 32)

    @block.gpsimd
    def _(pool):
        ser = Serial(pool, p_ser)
        ser.flag(nc.gpsimd.memset(epsc[:, :], EPS), "eps_set", 1)

        def split(u, q, slot):
            pool.wait_ge(raw[slot], q * 16 + 16)
            if not (isinstance(u, int) and u < 4):
                pool.wait_ge(unit, u - 3)
            nc.gpsimd.tensor_tensor(ptick[:, :], epsc[:, :], epsc[:, :], ALU.add)
            nc.gpsimd.tensor_scalar(w1[:, slot, :], w_raw[:, slot, :], 1.0, 1.0, ALU.mult, ALU.mult).then_inc(w_hi, 1)
            pool.wait_ge(w_hi, u + 1)
            nc.gpsimd.tensor_tensor(w2[:, slot, :], w_raw[:, slot, :], w1[:, slot, :].bitcast(F32), ALU.subtract).then_inc(w_lo, 1)
            pool.wait_ge(w_lo, u + 1)

        def norm(n):
            for k in range(0, KT, 2):
                pool.wait_ge(ev("norm_hi"), n * KT + k + 1)
                ser.flag(nc.gpsimd.tensor_tensor(h2[:, k, :], T[k % 4], h1[:, k, :].bitcast(F32), ALU.subtract),
                         "norm_lo_even", n * 4 + k // 2 + 1)

        norm(0)
        pool.wait_ge(ev("wif_hi"), 1)
        ser.flag(nc.gpsimd.tensor_tensor(wif2[:, :, :], wif[:, :, :], wif1[:, :, :].bitcast(F32), ALU.subtract), "wif_lo", 1)
        for u in range(4):
            split(u, 0, u)
        with nc.gpsimd.Fori(0, 3) as j:
            for i in range(4, 20):
                split(j * 16 + i, j * 4 + i // 4, i % 4)
        for u in range(52, 67):
            split(u, u // 4, u % 4)
        for k in range(KT):
            pool.wait_ge(ev("y_hi"), k + 1)
            ser.flag(nc.gpsimd.tensor_tensor(h2[:, k, :], y[:, k, :], h1[:, k, :].bitcast(F32), ALU.subtract), "y_lo", k + 1)
            split(u_out + 3 + k, (u_out + 3 + k) // 4, (k + 3) % 4)
        norm(1)

        def mlp(c, last):
            for i in range(16):
                if not last or i < 13:
                    split(c * 16 + (u_mlp + 3 + i), c * 4 + (u_mlp + 3 + i) // 4, (i + 3) % 4)

        with nc.gpsimd.Fori(0, 3) as c:
            mlp(c, False)
        mlp(3, True)

        for l in range(2):
            o = u_two + per_layer * l
            H0 = 8 * l

            def sp2(off, q=0):
                u = o + off
                split(q * 4 + u, q + u // 4, u % 4)

            def level(v, n):
                L = 64 >> n
                if n == 0:
                    pool.wait_ge(ev("b_ready"), v)
                if n >= 3:
                    pool.wait_ge(ev("level_mul"), v * 7 - 7 + n - 2)
                bv = bb[:, :].rearrange("p (m w) -> p m w", w=2 * L)
                ser.flag(nc.gpsimd.tensor_tensor(lev[:, n % 3, :].rearrange("p (m w) -> p m w", w=2 * L), bv,
                                                 bv[:, :, L - 1:L].broadcast_to([P, 256 // L, 2 * L]), ALU.subtract),
                         "level_x", v * 7 - 7 + n + 1)

            def half(j, b, units, mix):
                v = j * 2 + b + H0
                for i, ns in enumerate(((), (0, 1, 2), (3, 4), (5, 6), (), ())):
                    if units:
                        sp2(2 + 6 * b + i + 3, j * 3)
                    if mix:
                        for n in ns:
                            level(v, n)

            if l == 0:
                for i in range(3):
                    sp2(i)
            norm(2 + l)
            if l == 0:
                ser.flag(nc.gpsimd.memset(kt[:, :, :], 0.0), "kt_zero", 1)
            sp2(3)
            sp2(4)
            half(0, 0, True, False)
            with nc.gpsimd.Fori(0, 3) as j:
                half(j, 1, True, True)
                half(j + 1, 0, True, True)
            half(3, 1, True, True)
            half(4, 0, False, True)
            for k in range(2 * KT):
                pool.wait_ge(ev("y2_hi"), 16 * l + k + 1)
                ser.flag(nc.gpsimd.tensor_tensor(h2[:, k % 8, :], y[:, k, :], h1[:, k % 8, :].bitcast(F32), ALU.subtract),
                         "y2_lo", 16 * l + k + 1)
                if k < 2 * KT - 3 or l == 0:
                    sp2(50 + k + 3)
            for n in range(0, KT, 2):
                pool.wait_ge(ev("post_scaled"), 8 * l + n + 1)
                ser.flag(nc.gpsimd.tensor_tensor(x[:, n, :], x[:, n, :], y[:, n, :], ALU.add), "x_added_even", 4 * l + n // 2 + 1)

    @block.scalar
    def _(act):
        A = nc.scalar.activation
        ser = Serial(act, a_ser)
        nc.scalar.preload_act_table_set("natural_log_exp_and_others")
        act.wait_ge(ev("eps_set"), 1)

        def norm(n, tile_final=None):
            for k in range(KT):
                if tile_final is not None:
                    act.wait_ge(*tile_final(k))
                ser.flag(A(squares[:, k, :], x[:, k, :], ACT.Square), "norm_sq", n * KT + k + 1)
            act.wait_ge(ev("norm_sum"), n + 1)
            ser(A(rstd[:, :], norm_bank(n), ACT.Ln, scale=1.0 / DM, bias=epsc[:, :]))
            ser.flag(A(rstd[:, :], rstd[:, :], ACT.Exp, scale=-0.5), "norm_rstd", n + 1)
            for k in range(KT):
                act.wait_ge(ev("norm_h"), n * KT + k + 1)
                ser.flag(A(h1[:, k, :], T[k % 4], ACT.Copy), "norm_hi", n * KT + k + 1)

        def log_sigmoid_rest(dst, src):
            ser(A(dst, src, ACT.Abs))
            ser(A(dst, dst, ACT.Exp, scale=-1.0))
            return A(dst, dst, ACT.Ln, bias=1.0)

        act.wait_ge(ev("x_ready"), NT)
        norm(0)
        act.wait_ge(s_cst, 48)
        ser.flag(A(wif1[:, :, :], wif[:, :, :], ACT.Copy), "wif_hi", 1)
        act.wait_ge(ev("if_copied"), 1)
        ser.flag(log_sigmoid_rest(gt[:, :, :], ifs[:, :, 8:16]), "f_rest", 1)
        act.wait_ge(ev("bm_ready"), 1)
        ser.flag(A(e_row[:, :], e_row[:, :], ACT.Exp, scale=-1.0), "e_ready", 1)
        act.wait_ge(ev("negm_ready"), 1)
        act.dma_start(scr_m, m_row[:, :]).then_inc(s_scr, 16)
        act.dma_start(scr_e, e_row[:, :]).then_inc(s_scr, 16)
        act.wait_ge(s_scr, 32)
        base0 = ser.n

        def half(j, b, units, mix):
            hu = j * 2 + b
            hm1 = hu
            su, sm = b, 1 - b
            nu = 9 if b == 0 else 7
            i0 = 0 if b == 0 else 9

            def evacuate(i):
                u = j * 16 + (i0 + i)
                dst = [qb[su], kb[su], vb[su], va[su], oa[su], ga[su], gb[su], qpad[:, 3:3 + S], kpad[:, 3:3 + S]][i]
                act.wait_ge(unit, u + 1)
                if i in (5, 6):
                    ins = A(dst[:, :], G[(i0 + i) % 2], ACT.Identity, bias=curp[su][:, i - 4:i - 3])
                else:
                    ins = A(dst if i > 6 else dst[:, :], G[(i0 + i) % 2], ACT.Copy)
                ins.then_inc(evac, 1)
                act.wait_ge(evac, u + 1)
                if i in (3, 4):
                    act.wait_ge(ev("v_turned"), hu * 2 + (i - 2))
                    A((vb, va)[i - 3][su][:, :], G[(i0 + i - 1) % 2], ACT.Copy).then_inc(ev("v_copied"), 1)
                    act.wait_ge(ev("v_copied"), hu * 2 + (i - 2))

            if units:
                if not (isinstance(j, int) and j == 0 and b == 0):
                    act.wait_ge(ev("mix_done"), hu)
                act.wait_ge(ev("curp_ready"), hu + 1)
                act.dma_start(negm[su][:, :], scr_m[bass.ds(hu, 1), :].broadcast_to([P, S])).then_inc(ev(f"rows_in{su}"), 16)
                act.dma_start(ebc[su][:, :], scr_e[bass.ds(hu, 1), :].broadcast_to([P, S])).then_inc(ev(f"rows_in{su}"), 16)
            if mix:
                ser.at(base0 + (hu - 1) * 14)
            v = hu
            if mix:
                ser.flag(A(sq[:, 0, :], qb[sm][:, :], ACT.Square), "sq_ready", v * 3 - 2)
                ser.flag(A(sq[:, 1, :], kb[sm][:, :], ACT.Square), "sq_ready", v * 3 - 1)
            if units:
                evacuate(0)
            if mix:
                for n in range(2):
                    act.wait_ge(ev("sum_ready"), v * 3 - 2 + n)
                    r = (t0, t1)[n]
                    ser(A(r[:, :], M[3 + n], ACT.Ln, scale=1.0 / P, bias=epsc[:, :]))
                    ser.flag(A(r[:, :], r[:, :], ACT.Exp, scale=-0.5), "rstd_ready", v * 3 - 2 + n)
                if b == 1:
                    for n, (s_, d_) in enumerate(((qa, t2), (ka, t3))):
                        act.wait_ge(ev("conv_done"), j * 2 + n + 1)
                        A(d_[:, :], s_[:, :], ACT.Abs).then_inc(ev("conv_abs"), 1)
                        act.wait_ge(ev("conv_abs"), j * 2 + n + 1)
                        A(d_[:, :], d_[:, :], ACT.Exp, scale=-1.0).then_inc(ev("conv_exp"), 1)
                        act.wait_ge(ev("conv_exp"), j * 2 + n + 1)
                        ser.flag(A(d_[:, :], d_[:, :], ACT.Ln, bias=1.0), "conv_rest", j * 2 + n + 1)
                    for n, d_ in enumerate((t2, t3)):
                        act.wait_ge(ev("conv_ls"), j * 2 + n + 1)
                        ser.flag(A(d_[:, :], d_[:, :], ACT.Exp), "conv_sig", j * 2 + n + 1)
            if units:
                evacuate(1)
            if mix:
                act.wait_ge(ev("z_done"), v)
                for n, c in enumerate(ZPART):
                    ser(A(lbuf[:, c], FZ[:, c], ACT.Abs))
                    ser(A(lbuf[:, c], lbuf[:, c], ACT.Exp, scale=-1.0))
                    ser.flag(A(lbuf[:, c], lbuf[:, c], ACT.Ln, bias=1.0), "z_rest", v * 2 - 1 + n)
            if units:
                evacuate(2)
            if mix:
                for n, g in enumerate((oa[sm], ga[sm], gb[sm])):
                    d_ = (t0, t1, t2)[n]
                    if n == 0:
                        act.wait_ge(ev("qk_normed"), v * 2)
                    if n == 2 and b == 1:
                        act.wait_ge(ev("conv_ready"), j * 2 + 2)
                    ser(A(d_[:, :], g[:, :], ACT.Abs))
                    ser(A(d_[:, :], d_[:, :], ACT.Exp, scale=-1.0))
                    ser.flag(A(d_[:, :], d_[:, :], ACT.Ln, bias=1.0), "gate_rest", v * 3 - 2 + n)
            if mix:
                act.wait_ge(ev("suffix_done"), v)
                act.wait_ge(ev("a_diag"), v)
                ser.flag(A(wbuf[:, :], FZ[:, 0:1280], ACT.Exp), "a_ready", v)
            if units:
                evacuate(3)
            if units:
                evacuate(4)
            if mix:
                act.wait_ge(ev("d_diag"), v)
                act.wait_ge(ev("ob_done"), v)
                act.wait_ge(ev(f"rows_in{sm}"), (j * 32 if sm == 1 else j * 32 + 32) if b == 0 else j * 32 + 32)
                for i in range(3):
                    lo, hi = REG[i] + P, REG[i] + REGLEN[i]
                    A(wbuf[:, lo:hi], negm[sm][:, P * i + P:S], ACT.Exp, bias=curp[sm][:, 4 + i:5 + i]).then_inc(ev("d_off"), 1)
                    act.wait_ge(ev("d_off"), v * 3 - 2 + i)
                for n in range(2):
                    ins = A(diag(wbuf, n), lbuf[:, 256 * n:256 * n + 256].rearrange("p (n w) -> p n w", w=P), ACT.Exp)
                    if n == 0:
                        ser(ins)
                    else:
                        ser.flag(ins, "d_ready", v)
            if units:
                evacuate(5)
            if mix:
                act.wait_ge(ev("den_done"), v)
                ser.flag(A(t3[:, :], M[5], ACT.Abs), "den_abs", v)
                for n, d_ in enumerate((t0, t2)):
                    act.wait_ge(ev("gate_ls"), v * 2 - 1 + n)
                    A(d_[:, :], d_[:, :], ACT.Exp).then_inc(ev("gate_sig"), 1)
                    act.wait_ge(ev("gate_sig"), v * 2 - 1 + n)
                act.wait_ge(ev("h_ready"), v)
                ser.flag(A(sq[:, 0, :], va[sm][:, :], ACT.Square), "sq_ready", v * 3)
            if units:
                evacuate(6)
            if mix:
                act.wait_ge(ev("sum_ready"), v * 3)
                ser(A(t1[:, :], M[5], ACT.Ln, scale=1.0 / P, bias=epsc[:, :]))
                ser.flag(A(t1[:, :], t1[:, :], ACT.Exp, scale=-0.5), "rstd_ready", v * 3)
                assert ser.n == 14, ser.n
            if units and b == 0:
                evacuate(7)
                evacuate(8)

        half(0, 0, True, False)
        with nc.scalar.Fori(0, 3) as j:
            half(j, 1, True, True)
            half(j + 1, 0, True, True)
        half(3, 1, True, True)
        half(4, 0, False, True)
        act.wait_ge(ev("mix_done"), 9)
        act.wait_ge(unit, 64)
        for k in range(KT):
            ser.flag(A(h1[:, k, :], y[:, k, :], ACT.Copy), "y_hi", k + 1)
        norm(1, lambda k: (ev("x_added"), k + 1))

        act.wait_ge(ev("lb_diff"), 1)
        ser.at(0, ev("act_lb"))
        ser.flag(A(lbt[:, 2:4, :], lbt[:, 2:4, :], ACT.Exp), "lb_exp", 1)
        with nc.scalar.Fori(0, 4) as c:
            for i in range(8):
                act.wait_ge(ev("hidden"), c * 8 + i + 1)
                ser.flag(A(a1[:, i, :], hid[:, i % 2, :], ACT.Copy), "hid_hi", c * 8 + i + 1)

        def rest(d_, g):
            ser(A(d_, g, ACT.Abs))
            ser(A(d_, d_, ACT.Exp, scale=-1.0))
            return A(d_, d_, ACT.Ln, bias=1.0)

        def half2(l, j, b, units, mix):
            o = per_layer * l + 2 + 6 * b
            hu = j * 2 + b + 8 * l
            v = hu
            su, sm_ = b, 1 - b

            def evacuate(i):
                u = j * 12 + (u_two + o + i)
                act.wait_ge(unit, u + 1)
                A((hq, hf, hv, hz, aq, az)[i][su][:, :], G[i % 2], ACT.Copy).then_inc(evac, 1)
                act.wait_ge(evac, evac_of(u, l))
                if i == 3:
                    act.wait_ge(ev("hv_turned"), hu + 1)
                    A(hv[su][:, :], G[0], ACT.Copy).then_inc(ev("hv_copied"), 1)
                    act.wait_ge(ev("hv_copied"), hu + 1)
                if i == 3 and not mix:
                    act.wait_ge(ev("k_rotated"), l + 1)
                    for g in range(2):
                        for hh in range(2):
                            act.dma_start(kd[g][64 * hh:64 * hh + 64, :], arot[64 * g:64 * g + 64, :]).then_inc(ev("k_spread"), 16)

            if units and not (isinstance(j, int) and j == 0 and b == 0 and l == 0):
                act.wait_ge(ev("mix2_done"), hu)
            if mix:
                ser.at((hu - 1) * 29, ev("act_mix2_step"))
            if units:
                evacuate(0)
            if mix:
                act.wait_ge(ev("mix2_done"), v)
                ser.flag(rest(T[0], hf[sm_][:, :]), "f2_rest", v)
                ser.flag(rest(T[2], hq[sm_][:, :]), "q_rest", v)
                act.wait_ge(ev("f_ls"), v)
                ser(A(T[0], T[0], ACT.Exp))
                ser.flag(A(T[1], T[1], ACT.Exp), "f_sig", v)
                ser.flag(A(T[0], T[0], ACT.Ln, scale=curh[sm_][:, 0:1], bias=curh[sm_][:, 1:2]), "lnf", v)
                act.wait_ge(ev("q_ls"), v)
                ser.flag(A(T[2], T[2], ACT.Exp), "q_sig", v)
            if units:
                evacuate(1)

            def level(n):
                L = 64 >> n
                act.wait_ge(ev("level_x"), v * 7 - 7 + n + 1)
                xv = lev[:, n % 3, :].rearrange("p (m w) -> p m w", w=2 * L)
                ser(A(xv[:, :, 0:L], xv[:, :, 0:L], ACT.Exp, scale=-1.0))
                ser.flag(A(xv[:, :, L:2 * L], xv[:, :, L:2 * L], ACT.Exp), "level_exp", v * 7 - 7 + n + 1)

            if mix:
                act.wait_ge(ev("b_ready"), v)
                ser(A(qe[:, :], bb[:, P:S], ACT.Exp))
                for i in range(3):
                    ser(A(kg[:, P * i:P * i + P], bb[:, P * i:P * i + P], ACT.Exp, scale=-1.0, bias=bb[:, P * i + P - 1:P * i + P]))
                ser.flag(A(etot[:, :], bb[:, P - 1:S:P], ACT.Exp), "block_exp", v)
                for n in range(3):
                    level(n)
            if units:
                evacuate(2)
            if mix:
                act.wait_ge(ev("neg_max"), v)
                for g in range(8):
                    sc = ps[:, 2:6, :].rearrange("p b (n w) -> p (b n) w", w=256)[:, g, :]
                    ser(A(prob[:, g // 4, 256 * (g % 4):256 * (g % 4) + 256], sc, ACT.Exp, bias=sm[:, 1, g:g + 1],
                          accum_out=sm[:, 2, g:g + 1]))
                ser.flag(A(sm[:, 4, :], sm[:, 3, :], ACT.Exp), "att_exp", v)
                level(3)
                level(4)
            if units:
                evacuate(3)
            if mix:
                ser.flag(rest(T[0], hz[sm_][:, :]), "z2_rest", v * 2 - 1)
                ser.flag(rest(T[1], az[sm_][:, :]), "z2_rest", v * 2)
                act.wait_ge(ev("off_done"), v)
                ser.flag(A(p_off[:, :], ps[:, 2:4, :].rearrange("p b n -> p (b n)")[:, 0:768], ACT.Copy), "off_ready", v)
                level(5)
                level(6)
            if units:
                evacuate(4)
            if mix:
                for n in range(2):
                    act.wait_ge(ev("z2_ls"), v * 2 - 1 + n)
                    ser.flag(A(T[n], T[n], ACT.Exp), "z2_sig", v * 2 - 1 + n)
                for hh in range(2):
                    act.wait_ge(ev("p_turned"), v * 2 - 1 + hh)
                    ser.flag(A(prob[:, hh, P:1024], ps[:, 2 + 2 * hh:4 + 2 * hh, :].rearrange("p b n -> p (b n)")[:, P:1024], ACT.Copy),
                             "pt_ready", v * 2 - 1 + hh)
            if units:
                evacuate(5)
            if mix:
                act.wait_ge(ev("o_done"), v)
                ser.flag(A(T[2], M[4], ACT.Square), "o_sq", v)
                act.wait_ge(ev("o_sum"), v)
                ser(A(T[2], M[5], ACT.Ln, scale=1.0 / P, bias=epsc[:, :]))
                ser.flag(A(T[2], T[2], ACT.Exp, scale=-0.5), "o_rstd", v)
                assert ser.n == 29, ser.n

        for l in range(2):
            o = per_layer * l
            norm(2 + l, (lambda k: (ev("mlp_evac"), 59 + k)) if l == 0 else (lambda k: x_added(0, k)))
            for i in range(2):
                u = u_two + o + i
                act.wait_ge(unit, u + 1)
                A((T[0], av[:, :])[i], G[i], ACT.Copy).then_inc(evac, 1)
                act.wait_ge(evac, evac_of(u, l))
                if i == 0:
                    A(T[1], T[0], ACT.Copy).then_inc(ev("k_copied"), 1)
                    act.wait_ge(ev("k_copied"), l + 1)
            act.wait_ge(ev("av_turned"), l + 1)
            A(av[:, :], M[0], ACT.Copy).then_inc(ev("av_copied"), 1)
            act.wait_ge(ev("av_copied"), l + 1)
            half2(l, 0, 0, True, False)
            with nc.scalar.Fori(0, 3) as j:
                half2(l, j, 1, True, True)
                half2(l, j + 1, 0, True, True)
            half2(l, 3, 1, True, True)
            half2(l, 4, 0, False, True)
            act.wait_ge(ev("mix2_done"), 8 * l + 9)
            act.wait_ge(unit, u_two + o + 50)
            for k in range(2 * KT):
                if k >= KT:
                    act.wait_ge(unit, u_two + o + 50 + k - 7)
                ser.flag(A(h1[:, k % 8, :], y[:, k, :], ACT.Copy), "y2_hi", 16 * l + k + 1)
            for n in range(KT):
                act.wait_ge(ev("post_copy"), 8 * l + n + 1)
                ser.flag(A(squares[:, n, :], y[:, n, :], ACT.Square), "post_sq", 8 * l + n + 1)
            act.wait_ge(ev("post_sum"), l + 1)
            ser.at(l, ev("act_post_step"))
            ser(A(rstd[:, :], G[0], ACT.Ln, scale=1.0 / DM, bias=epsc[:, :]))
            ser.flag(A(rstd[:, :], rstd[:, :], ACT.Exp, scale=-0.5), "post_rstd", l + 1)
            if l == 0:
                ser.at(l, ev("act_norm3_step"))

    @block.tensor
    def _(pe):
        mm = nc.tensor.matmul

        def product(o, l1, l2, r1, r2, start, stop):
            mm(o, l1, r1, start=start, stop=False)
            mm(o, l1, r2, start=False, stop=False)
            return mm(o, l2, r1, start=False, stop=stop)

        def feature_unit(u, slot, o, act1, act2, tile_ready=None):
            pe.wait_ge(w_lo, u + 1)
            for k in range(KT):
                if tile_ready is not None:
                    pe.wait_ge(*tile_ready(k))
                W1, W2 = w1[:, slot, P * k:P * k + P], w2[:, slot, P * k:P * k + P]
                last = product(o, W1, W2, act1[:, k, :], act2[:, k, :], k == 0, k == KT - 1)
            last.then_inc(unit, 1)

        def turn(bank, tile, flag):
            for n in range(NT):
                last = nc.tensor.transpose(bank[:, P * n:P * n + P], tile[:, P * n:P * n + P], ident)
            last.then_inc(flag, 1)

        def norm_tile(n, k):
            pe.wait_ge(ev("norm_sq"), n * KT + k + 1)
            ins = mm(norm_bank(n), ones, squares[:, k, :], start=k == 0, stop=k == KT - 1)
            if k == KT - 1:
                ins.then_inc(ev("norm_sum"), 1)

        def norm(n):
            for k in range(KT):
                norm_tile(n, k)

        pe.wait_ge(s_cst, 48)
        for n in range(NT):
            pe.wait_ge(ev(f"x_loaded{n}"), 16)
            if n >= 2:
                pe.wait_ge(ev("x_ready"), n - 1)
            for k in range(KT):
                last = nc.tensor.transpose(M[2 * (n % 2) + k // 4][:, P * (k % 4):P * (k % 4) + P], xin[:, n, P * k:P * k + P], ident)
            last.then_inc(ev("x_t"), 1)
        pe.wait_ge(s_rows, 176)
        nc.tensor.transpose(M[4][:, 0:R_END], rows[0:R_END, :], cst[0:R_END, K_ID:K_ID + R_END]).then_inc(ev("par_t"), 1)
        pe.wait_ge(ev("par_ready"), 1)
        norm(0)
        for k in range(6, KT):
            pe.wait_ge(*norm_lo(0, k))
        pe.wait_ge(ev("wif_lo"), 1)
        for m in range(NT):
            o = M[0][:, 16 * m:16 * m + 16]
            tk = slice(P * m, P * m + P)
            for k in range(KT):
                product(o, h1[:, k, tk], h2[:, k, tk], wif1[:, k, :], wif2[:, k, :], k == 0, False)
            last = mm(o, cst[0:1, K_ONES:K_ONES + P], bif[:, :], start=False, stop=True)
        last.then_inc(ev("if_done"), 1)
        pe.wait_ge(ev("logf_ready"), 1)
        for n in range(NT):
            o = M[1][:, 8 * n:8 * n + 8]
            for i in range(n + 1):
                last = mm(o, cst[:, K_TRI:K_TRI + P] if i == n else ones, logf[:, i, :], start=i == 0, stop=i == n)
        last.then_inc(ev("b_done"), 1)
        pe.wait_ge(ev("c_ready"), 1)
        for n in range(NT):
            nc.tensor.transpose(M[2][0:8, P * n:P * n + P], c_tok[:, n, :], ident)
            last = nc.tensor.transpose(M[3][0:8, P * n:P * n + P], b_tok[:, n, :], ident)
        last.then_inc(ev("cb_t"), 1)

        def half(j, b, units, mix):
            hu = j * 2 + b
            v = hu
            su, sm = b, 1 - b
            i0 = 0 if b == 0 else 9

            def unit_i(i):
                u = j * 16 + (i0 + i)
                if not (isinstance(u, int) and u < 2):
                    pe.wait_ge(evac, u - 1)
                if i in (4, 5):
                    pe.wait_ge(ev("v_copied"), hu * 2 + (i - 3))
                feature_unit(u, (i0 + i) % 4, G[(i0 + i) % 2], h1, h2)
                if i in (3, 4):
                    pe.wait_ge(evac, u)
                    turn(G[(i0 + i - 1) % 2], (vb, va)[i - 3][su], ev("v_turned"))

            po = 64 * sm
            if units:
                unit_i(0)
            if mix:
                pe.wait_ge(ev("mix_done"), v)
                for n in range(2):
                    pe.wait_ge(ev("sq_ready"), v * 3 - 2 + n)
                    mm(M[3 + n], ones, sq[:, n, :], start=True, stop=True).then_inc(ev("sum_ready"), 1)
            if units:
                unit_i(1)
            if mix:
                pe.wait_ge(ev("qk_normed"), v * 2)
                for i in (0, 1, 3, 2):
                    last = mm(FZ[:, REG[i]:REG[i] + REGLEN[i]], kb[sm][:, P * i:P * i + P], qb[sm][:, P * i:S],
                              start=i != 3, stop=True, skip_group_check=True)
                last.then_inc(ev("z_done"), 1)
            if units:
                unit_i(2)
            if mix:
                pe.wait_ge(ev("l_ready"), v)
                for i in range(NT):
                    for jb in range(i, NT):
                        d = P * (jb - i)
                        last = mm(FZ[:, REG[i] + d:REG[i] + REGLEN[i]],
                                  cst[:, K_NEGTRI:K_NEGTRI + P] if jb == i else cst[:, K_NEGONES:K_NEGONES + P],
                                  lbuf[:, REG[jb]:REG[jb] + REGLEN[jb]], start=False, stop=True, skip_group_check=True)
                last.then_inc(ev("suffix_done"), 1)
            if units:
                unit_i(3)
            if mix:
                pe.wait_ge(ev("a_ready"), v)
                for i in range(NT):
                    last = mm(M[3][:, P * i:S], vb[sm][:, P * i:P * i + P], wbuf[:, REG[i]:REG[i] + REGLEN[i]],
                              start=i == 0, stop=i == NT - 1)
                last.then_inc(ev("ob_done"), 1)
            if units:
                unit_i(4)
            if mix:
                pe.wait_ge(ev("conv_ready"), (j * 2 + 2) if b == 1 else j * 2)
                for i in (0, 1, 3, 2):
                    last = mm(FZ[:, REG[i]:REG[i] + REGLEN[i]], ka[po:po + 64, P * i:P * i + P], qa[po:po + 64, P * i:S],
                              start=i != 3, stop=True, skip_group_check=True)
                last.then_inc(ev("s_done"), 1)
            if units:
                unit_i(5)
            if mix:
                pe.wait_ge(ev("p_ready"), v)
                for o, l in ((M[5], ones), (M[4], None)):
                    for i in range(NT):
                        last = mm(o[:, P * i:S], va[sm][:, P * i:P * i + P] if l is None else l,
                                  wbuf[:, REG[i]:REG[i] + REGLEN[i]], start=i == 0, stop=i == NT - 1)
                    last.then_inc(ev("den_done" if l is ones else "num_done"), 1)
            if units:
                unit_i(6)
            if mix:
                pe.wait_ge(ev("sq_ready"), v * 3)
                mm(M[5], ones, sq[:, 0, :], start=True, stop=True).then_inc(ev("sum_ready"), 1)
            if units and b == 0:
                unit_i(7)
                unit_i(8)

        half(0, 0, True, False)
        with nc.tensor.Fori(0, 3) as j:
            half(j, 1, True, True)
            half(j + 1, 0, True, True)
        half(3, 1, True, True)
        half(4, 0, False, True)
        pe.wait_ge(ev("mix_done"), 9)
        pe.wait_ge(evac, 64)
        for k in range(KT):
            pe.wait_ge(w_lo, u_out + k + 1)
            pe.wait_ge(ev("y_lo"), k + 1)
            for n in range(KT):
                W1, W2 = w1[:, k % 4, P * n:P * n + P], w2[:, k % 4, P * n:P * n + P]
                last = product(ps[:, n, :], W1, W2, h1[:, k, :], h2[:, k, :], k == 0, k == KT - 1)
                if k == KT - 1 and n < KT - 1:
                    last.then_inc(ev("bank_done"), 1)
            last.then_inc(unit, 1)
        norm(1)
        def mlp(c, last, first=False):
            for i in range(16):
                pe.wait_ge(ev("mlp_evac"), c * 16 + i + 1)
                ready = (lambda k: norm_lo(1, k)) if first and i == 0 else (lambda k: (ev("hid_lo"), c * 8 + k + 1)) if i == 8 else None
                feature_unit(c * 16 + (u_mlp + i), i % 4, G[i % 2], *((h1, h2) if i < 8 else (a1, a2)), tile_ready=ready)
                if last and i > 8:
                    norm_tile(2, i - 9)

        mlp(0, False, True)
        with nc.tensor.Fori(1, 3) as c:
            mlp(c, False)
        mlp(3, True)
        norm_tile(2, 7)
        for l in range(2):
            o = u_two + per_layer * l
            H0 = 8 * l

            def item(v, n, kl, qr, width):
                bank = M[4 + n % 2]
                if n >= 2:
                    pe.wait_ge(ev("item_used"), v * 8 - 8 + n - 1)
                for m in range(NT):
                    last = mm(bank[:, width * m:width * m + width], kl[:, P * m:P * m + P], qr[:, width * m:width * m + width],
                              start=True, stop=True)
                last.then_inc(ev("item_done"), 1)

            def level(v, n, s_):
                pe.wait_ge(ev("level_mul"), v * 7 - 7 + n + 1)
                item(v, n + 1, kt[:, n % 2, :], qt[:, n % 2, :], 64)

            def half2(j, b, units, mix):
                v = j * 2 + b + H0
                s_ = 1 - b
                g = s_
                kd_ = kd[g]

                def unit_i(i):
                    u = j * 12 + (o + 2 + 6 * b + i)
                    pe.wait_ge(evac, evac_of(u - 2, l))
                    if i == 4:
                        pe.wait_ge(ev("hv_copied"), v + 1)
                    feature_unit(u, (o + 2 + 6 * b + i) % 4, G[i % 2], h1, h2)
                    if i == 3:
                        pe.wait_ge(evac, evac_of(u - 1, l))
                        turn(G[0], hv[b], ev("hv_turned"))

                if units:
                    unit_i(0)
                if mix:
                    pe.wait_ge(ev("mix2_done"), v)
                    mm(M[4], cst[:, K_ROT:K_ROT + P], aq[s_][:, :], start=True, stop=True).then_inc(ev("q_turned"), 1)
                if units:
                    unit_i(1)
                if mix:
                    pe.wait_ge(ev("q_rotated"), v)
                    for hh in range(2):
                        po = 64 * hh
                        for n in range(NT):
                            out_ = ps[:, 2 + 2 * hh + n // 2, 256 * (n % 2):256 * (n % 2) + 256]
                            mm(out_, identb[:, :], wmask[:, min(n, 1), :], start=n % 2 == 0, stop=True, skip_group_check=True)
                            lo = P if n == 0 else 0
                            last = mm(out_[:, lo:256], aq[s_][po:po + 64, P * n:P * n + P],
                                      kd_[po:po + 64, P * (n - 1) + lo:P * (n + 1)], start=False, stop=True,
                                      skip_group_check=True)
                    last.then_inc(ev("scores_done"), 1)
                    pe.wait_ge(ev("qk_ready"), v)
                    item(v, 0, kk[:, :], hq[s_][:, :], P)
                if units:
                    unit_i(2)
                if mix:
                    level(v, 0, s_)
                    level(v, 1, s_)
                if units:
                    unit_i(3)
                if mix:
                    pe.wait_ge(ev("att_exp"), v)
                    pe.wait_ge(ev("block_mul"), v)
                    off = ps[:, 2:4, :].rearrange("p b n -> p (b n)")
                    for ka_, to, src in ((0, 0, qe[:, 0:P]), (0, P, xe[:, 0:P]), (0, 2 * P, xe[:, 256:384]), (2, 384, qe[:, 256:384]),
                                         (1, 512, qe[:, P:256]), (1, 640, xe[:, P:256])):
                        last = mm(off[:, to:to + P], kg[:, P * ka_:P * ka_ + P], src, start=to in (0, 512), stop=True,
                                  skip_group_check=True)
                    last.then_inc(ev("off_done"), 1)
                    level(v, 2, s_)
                    level(v, 3, s_)
                if units:
                    unit_i(4)
                if mix:
                    pe.wait_ge(ev("p_normed"), v)
                    pe.wait_ge(ev("off_ready"), v)
                    for hh in range(2):
                        for n in range(NT):
                            for part in ((1,) if n == 0 else (0, 1)):
                                c = 256 * n + P * part
                                last = nc.tensor.transpose(ps[:, 2 + 2 * hh + c // 512, c % 512:c % 512 + P],
                                                           prob[:, hh, c:c + P], ident)
                        last.then_inc(ev("p_turned"), 1)
                    level(v, 4, s_)
                    level(v, 5, s_)
                if units:
                    unit_i(5)
                if mix:
                    level(v, 6, s_)
                    pe.wait_ge(ev("pt_ready"), v * 2)

                    def att(hh):
                        for n in range(NT):
                            out_ = M[2][64 * hh:64 * hh + 64, P * n:P * n + P]
                            last = mm(out_, av[:, P * n + 64 * g:P * n + 64 * g + 64], prob[:, hh, 256 * n + P:256 * n + 256],
                                      start=True, stop=n == 0)
                            if n:
                                last = mm(out_, av[:, P * (n - 1) + 64 * g:P * (n - 1) + 64 * g + 64],
                                          prob[:, hh, 256 * n:256 * n + P], start=False, stop=True)
                        return last

                    att(0)
                    pe.wait_ge(ev("item_used"), v * 8)
                    for n in range(NT):
                        mm(M[4][:, P * n:P * n + P], hv[s_][:, P * n:P * n + P], p_diag[:, P * n:P * n + P], start=n == 0,
                           stop=False, skip_group_check=True)
                    for i in range(3):
                        last = mm(M[4][:, P * (i + 1):S], hv[s_][:, P * i:P * i + P], p_off[:, OFF[i]:OFF[i] + S - P * (i + 1)],
                                  start=False, stop=i == 2, skip_group_check=True)
                    last.then_inc(ev("o_done"), 1)
                    att(1).then_inc(ev("att_done"), 1)
                    pe.wait_ge(ev("o_sq"), v)
                    mm(M[5], ones, T[2], start=True, stop=True).then_inc(ev("o_sum"), 1)

            if l == 1:
                norm(3)
            feature_unit(o, o % 4, G[0], h1, h2, tile_ready=lambda k: norm_lo(2 + l, k))
            feature_unit(o + 1, (o + 1) % 4, G[1], h1, h2)
            pe.wait_ge(ev("k_copied"), l + 1)
            mm(M[4], cst[:, K_ROT:K_ROT + P], T[1], start=True, stop=True).then_inc(ev("k_turned"), 1)
            pe.wait_ge(evac, evac_of(o + 1, l))
            turn(M[0], av, ev("av_turned"))
            half2(0, 0, True, False)
            pe.wait_ge(ev("k_spread"), 64 * (l + 1))
            with nc.tensor.Fori(0, 3) as j:
                half2(j, 1, True, True)
                half2(j + 1, 0, True, True)
            half2(3, 1, True, True)
            half2(4, 0, False, True)
            pe.wait_ge(ev("mix2_done"), 8 * l + 9)
            pe.wait_ge(evac, evac_of(o + 49, l))
            for k in range(2 * KT):
                pe.wait_ge(w_lo, o + 50 + k + 1)
                pe.wait_ge(ev("y2_lo"), 16 * l + k + 1)
                for n in range(KT):
                    W1, W2 = w1[:, (o + 50 + k) % 4, P * n:P * n + P], w2[:, (o + 50 + k) % 4, P * n:P * n + P]
                    last = product(ps[:, n, :], W1, W2, h1[:, k % 8, :], h2[:, k % 8, :], k == 0, k == 2 * KT - 1)
                    if k == 2 * KT - 1 and n < KT - 1:
                        last.then_inc(ev("bank_done"), 1)
                last.then_inc(unit, 1)
            pe.wait_ge(ev("post_copy"), 8 * l + 1)
            for n in range(KT):
                pe.wait_ge(ev("post_sq"), 8 * l + n + 1)
                last = mm(G[0], ones, squares[:, n, :], start=n == 0, stop=n == KT - 1)
            last.then_inc(ev("post_sum"), 1)
        for half_ in range(2):
            for k in range(4 * half_, 4 * half_ + 4):
                pe.wait_ge(*x_added(1, k))
            for n in range(NT):
                m = 4 * half_ + n
                if m >= 4:
                    pe.wait_ge(ev("out_rows"), m - 3)
                for i in range(4):
                    last = nc.tensor.transpose(M[m % 4][:, P * i:P * i + P], x[:, 4 * half_ + i, P * n:P * n + P], ident)
                last.then_inc(ev("out_t"), 1)

    @block.vector
    def _(dve):
        V = nc.vector
        ser = Serial(dve, d_ser)
        TT, TS, STT = V.tensor_tensor, V.tensor_scalar, V.scalar_tensor_tensor
        ser(V.memset(qpad[:, 0:3], 0.0))
        ser(V.memset(kpad[:, 0:3], 0.0))
        V.memset(tick[:, 0:1], 0.0).then_inc(ev("mix_done"), 1)
        for n in range(NT):
            dve.wait_ge(ev("x_t"), n + 1)
            ser.flag(V.tensor_copy(x[:, :, P * n:P * n + P], ps[:, 2 + 2 * (n % 2):4 + 2 * (n % 2), :].rearrange("p b (k t) -> p (b k) t", t=P)),
                     "x_ready", n + 1)
        dve.wait_ge(ev("par_t"), 1)
        ser(V.tensor_copy(par[:, 0:R_END], M[4][:, 0:R_END]))
        ser.flag(TS(par[:, R_SBQ:R_SBQ + 1], par[:, R_SBQ:R_SBQ + 1], float(P) ** -0.5, None, ALU.mult), "par_ready", 1)

        def norm(n, r):
            dve.wait_ge(ev("norm_rstd"), n + 1)
            for k in range(KT):
                if k >= 4 and k % 2 == 0:
                    dve.wait_ge(*norm_lo(n, k - 4))
                ser.flag(STT(T[k % 4], x[:, k, :], par[:, r + k:r + k + 1], rstd[:, :], ALU.mult, ALU.mult),
                         "norm_h", n * KT + k + 1)
                if k % 2 == 0 and k > 0:
                    lo(n, k - 1)
            lo(n, KT - 1)

        def lo(n, k):
            dve.wait_ge(ev("norm_hi"), n * KT + k + 1)
            ser.flag(TT(h2[:, k, :], T[k % 4], h1[:, k, :].bitcast(F32), ALU.subtract), "norm_lo_odd", n * 4 + k // 2 + 1)

        norm(0, R_NMIX)
        dve.wait_ge(ev("if_done"), 1)
        ser.flag(V.tensor_copy(ifs[:, :, :], M[0][:, 0:64].rearrange("p (n c) -> p n c", n=NT)), "if_copied", 1)
        dve.wait_ge(ev("f_rest"), 1)
        ser.flag(STT(logf[:, :, :], ifs[:, :, 8:16], 0.0, gt[:, :, :], ALU.min, ALU.subtract), "logf_ready", 1)
        dve.wait_ge(ev("b_done"), 1)
        ser(V.tensor_copy(b_tok[:, :, :], M[1][:, 0:32].rearrange("p (n c) -> p n c", n=NT)))
        ser.flag(TT(c_tok[:, :, :], ifs[:, :, 0:8], b_tok[:, :, :], ALU.subtract), "c_ready", 1)
        dve.wait_ge(ev("cb_t"), 1)
        ser(V.tensor_copy(c_row[:, :], M[2][0:8, :]))
        ser(V.tensor_tensor_scan(m_row[:, :], c_row[:, :], c_row[:, :], 0.0, ALU.max, ALU.max))
        ser.flag(TT(e_row[:, :], M[3][0:8, :], m_row[:, :], ALU.add), "bm_ready", 1)
        ser.flag(TS(m_row[:, :], m_row[:, :], -1.0, None, ALU.mult), "negm_ready", 1)
        base0 = ser.n

        def half(j, b, units, mix):
            hu = j * 2 + b
            v = hu
            su, sm = b, 1 - b
            if units:
                cp = curp[su]
                ser.at(base0 + hu * 3)
                ser(V.tensor_copy(cp[:, 0:1], par[:, bass.ds(hu + R_MG, 1)]))
                ser(V.tensor_copy(cp[:, 1:3], par[:, bass.ds(hu + R_BGATE, 2, 8)]))
                ser(V.tensor_copy(cp[:, 4:8], c_tok[:, :, bass.ds(hu, 1)].rearrange("p n c -> p (n c)")))
                TS(cp[:, 3:4], cp[:, 0:1], 1.0, None, ALU.mult).then_inc(ev("curp_ready"), 1)
                dve.wait_ge(ev("curp_ready"), hu + 1)
            if not mix:
                return
            mser = Serial(dve, ev("dve_mix_step"))
            mser.at((hu - 1) * 11)
            cser = Serial(dve, ev("dve_conv_step"))
            if b == 1:
                cser.at(j * 7)
                cser(V.tensor_copy(convp[:, :], par[:, bass.ds(j + R_CONV, 8, 4)]))
                dve.wait_ge(evac, j * 16 + 9)
                for n, (pad, dst) in enumerate(((qpad, qa), (kpad, ka))):
                    w = lambda tap: convp[:, 2 * tap + n:2 * tap + n + 1]
                    cser(TS(dst[:, :], pad[:, 0:S], w(0), None, ALU.mult))
                    for tap in (1, 2):
                        cser(STT(dst[:, :], pad[:, tap:tap + S], w(tap), dst[:, :], ALU.mult, ALU.add))
                    cser.flag(STT(dst[:, :], pad[:, 3:3 + S], w(3), dst[:, :], ALU.mult, ALU.add), "conv_done", j * 2 + n + 1)
            for n, (tile, g) in enumerate(((qb[sm], R_SBQ), (kb[sm], R_SBK))):
                dve.wait_ge(ev("rstd_ready"), v * 3 - 2 + n)
                mser.flag(STT(tile[:, :], tile[:, :], par[:, g:g + 1], (t0, t1)[n][:, :], ALU.mult, ALU.mult), "qk_normed", v * 2 - 1 + n)
            if b == 1:
                for n, (s_, d_) in enumerate(((qa, t2), (ka, t3))):
                    dve.wait_ge(ev("conv_rest"), j * 2 + n + 1)
                    cser.flag(STT(d_[:, :], s_[:, :], 0.0, d_[:, :], ALU.min, ALU.subtract), "conv_ls", j * 2 + n + 1)
                for n, (s_, d_) in enumerate(((qa, t2), (ka, t3))):
                    dve.wait_ge(ev("conv_sig"), j * 2 + n + 1)
                    cser.flag(STT(s_[:, :], s_[:, :], (1.0, 0.125)[n], d_[:, :], ALU.mult, ALU.mult), "conv_ready", j * 2 + n + 1)
                assert cser.n == 7
            for n, c in enumerate(ZPART):
                dve.wait_ge(ev("z_rest"), v * 2 - 1 + n)
                mser(STT(lbuf[:, c], FZ[:, c], 0.0, lbuf[:, c], ALU.max, ALU.add))
            for n in range(2):
                ins = TT(diag(lbuf, n), diag(lbuf, n), mask2(K_STRICT), ALU.mult)
                if n == 0:
                    mser(ins)
                else:
                    mser.flag(ins, "l_ready", v)
            for n, g in enumerate((oa[sm], ga[sm], gb[sm])):
                d_ = (t0, t1, t2)[n]
                dve.wait_ge(ev("gate_rest"), v * 3 - 2 + n)
                ins = STT(d_[:, :], g[:, :], 0.0, d_[:, :], ALU.min, ALU.subtract)
                if n < 2:
                    mser(ins)
                if n == 1:
                    mser.flag(TT(t0[:, :], t0[:, :], t1[:, :], ALU.add), "gate_ls", v * 2 - 1)
                if n == 2:
                    mser.flag(ins, "gate_ls", v * 2)
            dve.wait_ge(ev("suffix_done"), v)
            for n in range(2):
                ins = STT(diag(FZ, n), diag(FZ, n), 0.0, mask2(K_SNEG), ALU.min, ALU.add)
                if n == 0:
                    mser(ins)
                else:
                    mser.flag(ins, "a_diag", v)
            dve.wait_ge(ev(f"rows_in{sm}"), (j * 32 if sm == 1 else j * 32 + 32) if b == 0 else j * 32 + 32)
            for i in range(NT):
                at = P * (0, 1, 3, 2)[i]
                ins = STT(lbuf[:, at:at + P], negm[sm][:, P * i:P * i + P], curp[sm][:, 4 + i:5 + i],
                          cst[:, K_CNEG:K_CNEG + P], ALU.add, ALU.add)
                if i < 3:
                    mser(ins)
                else:
                    mser.flag(ins, "d_diag", v)
            dve.wait_ge(ev("s_done"), v)
            dve.wait_ge(ev("d_ready"), v)
            mser.flag(TT(wbuf[:, :], wbuf[:, :], FZ[:, 0:1280], ALU.mult), "p_ready", v)
            dve.wait_ge(ev("den_abs"), v)
            mser(TT(t3[:, :], t3[:, :], ebc[sm][:, :], ALU.max))
            mser(V.reciprocal(t3[:, :], t3[:, :]))
            dve.wait_ge(ev("num_done"), v)
            mser.flag(TT(va[sm][:, :], M[4], t3[:, :], ALU.mult), "h_ready", v)
            dve.wait_ge(ev("rstd_ready"), v * 3)
            dve.wait_ge(ev("gate_sig"), v * 2)
            D2 = Serial(dve, ev("dve_tail_step"))
            D2.at((hu - 1) * 3)
            D2(STT(t1[:, :], va[sm][:, :], curp[sm][:, 0:1], t1[:, :], ALU.mult, ALU.mult))
            D2(TT(t1[:, :], t1[:, :], t0[:, :], ALU.mult))
            D2(TT(t2[:, :], M[3], t2[:, :], ALU.mult))
            D2.flag(TT(y[:, bass.ds(hu - 1, 1), :].rearrange("p a n -> p (a n)"), t1[:, :], t2[:, :], ALU.add), "mix_done", v + 1)
            assert mser.n == 11, mser.n

        half(0, 0, True, False)
        with nc.vector.Fori(0, 3) as j:
            half(j, 1, True, True)
            half(j + 1, 0, True, True)
        half(3, 1, True, True)
        half(4, 0, False, True)
        ser.at(base0 + 24)
        for n in range(KT):
            dve.wait_ge(*((ev("bank_done"), n + 1) if n < 7 else (unit, 72)))
            ser.flag(TT(x[:, n, :], x[:, n, :], ps[:, n, :], ALU.add), "x_added", n + 1)
        for n in range(2):
            V.memset(tick[:, 1:2], 0.0).then_inc(ev("mlp_evac"), 1)
            dve.wait_ge(ev("mlp_evac"), n + 1)
        norm(1, R_NMLP)
        dve.wait_ge(ev("consts2"), 48)
        ser.at(0, ev("dve_setup2"))
        V.memset(tick[:, 2:3], 0.0).then_inc(ev("mix2_done"), 1)
        ser(V.tensor_copy(lmask[:, :, :].rearrange("p l (n w) -> p l n w", n=NT),
                          prob[:, 0, 0:448].rearrange("p (l w) -> p l w", l=7).unsqueeze(2).broadcast_to([P, 7, NT, 64])))
        ser(V.tensor_copy(wmask[:, :, :], prob[:, 0, 448:960].rearrange("p (a w) -> p a w", a=2)))
        ser(V.tensor_copy(identb[:, :], ident))
        ser(V.memset(lnc[:, :], LNC))
        a0, a1_ = par[:, R_LB:R_LB + 8], par[:, R_LB + 8:R_LB + 16]
        ser(TT(lbt[:, 0, :], a0, a1_, ALU.max))
        ser(TT(lbt[:, 2, :], a0, lbt[:, 0, :], ALU.subtract))
        ser.flag(TT(lbt[:, 3, :], a1_, lbt[:, 0, :], ALU.subtract), "lb_diff", 1)
        dve.wait_ge(ev("lb_exp"), 1)
        ser(TT(lbt[:, 0, :], lbt[:, 2, :], lbt[:, 3, :], ALU.add))
        ser(V.reciprocal(lbt[:, 1, :], lbt[:, 0, :]))
        ser(TT(lbt[:, 2, :], lbt[:, 2, :], lbt[:, 1, :], ALU.mult))
        ser(TT(lbt[:, 3, :], lbt[:, 3, :], lbt[:, 1, :], ALU.mult))
        ser(TT(lbt[:, 3, :], lbt[:, 2, :], lbt[:, 3, :], ALU.add))
        ser(TT(lbt[:, 4, :], lbt[:, 2, :], lbt[:, 2, :], ALU.subtract))
        ser(TT(lbt[:, 5, :], lbt[:, 3, :], lbt[:, 2, :], ALU.subtract))
        for l in range(2):
            lb = lbt[:, 4 + l, :]
            ser(TS(lbt[:, 0, :], lb, 1e-20, None, ALU.max))
            ser(TS(lbp[:, l, 2, :], lb, -1.0, 1.0, ALU.mult, ALU.add))
            ser(TS(lbp[:, l, 0, :], lbp[:, l, 2, :], LNS, None, ALU.mult))
            ser(TS(lbp[:, l, 1, :], lbt[:, 0, :], LNS, None, ALU.mult))
            ser(TT(lbp[:, l, 3, :], lbt[:, 0, :], lb, ALU.subtract))
        with nc.vector.Fori(0, 4) as c:
            for i in range(16):
                dve.wait_ge(unit, c * 16 + (u_mlp + i + 1))
                if i < 8:
                    V.tensor_scalar(hid[:, i % 2, :], G[i % 2], 0.0, None, ALU.max).then_inc(ev("mlp_evac"), 1)
                    dve.wait_ge(ev("mlp_evac"), c * 16 + i + 3)
                    V.tensor_tensor(hid[:, i % 2, :], hid[:, i % 2, :], hid[:, i % 2, :], ALU.mult).then_inc(ev("hidden"), 1)
                    dve.wait_ge(ev("hidden"), c * 8 + i + 1)
                    dve.wait_ge(ev("hid_hi"), c * 8 + i + 1)
                    TT(a2[:, i, :], hid[:, i % 2, :], a1[:, i, :].bitcast(F32), ALU.subtract).then_inc(ev("hid_lo"), 1)
                    dve.wait_ge(ev("hid_lo"), c * 8 + i + 1)
                else:
                    TT(x[:, i - 8, :], x[:, i - 8, :], G[i % 2], ALU.add).then_inc(ev("mlp_evac"), 1)
                    dve.wait_ge(ev("mlp_evac"), c * 16 + i + 3)
        def half2(l, j, b, units, mix):
            hu = j * 2 + b + 8 * l
            v = hu
            su, s_ = b, 1 - b
            if units:
                cp = curh[su]
                ser.at(hu * 1, ev("dve_cur2_step"))
                ser(V.tensor_copy(cp[:, 0:4], lbp[:, l, :, bass.ds(j * 2 + b, 1)].rearrange("p n c -> p (n c)")))
                V.tensor_copy(cp[:, 4:6], sinkb[:, bass.ds(j * 2 + (16 * l + 8 * b), 2)]).then_inc(ev("curh_ready"), 1)
                dve.wait_ge(ev("curh_ready"), hu + 1)
            if not mix:
                return
            ser.at((hu - 1) * 34, ev("dve_mix2_step"))
            q_, f_ = hq[s_][:, :], hf[s_][:, :]
            dve.wait_ge(ev("f2_rest"), v)
            ser(STT(T[0], f_, 0.0, T[0], ALU.min, ALU.subtract))
            ser.flag(TT(T[1], T[0], f_, ALU.subtract), "f_ls", v)
            dve.wait_ge(ev("q_turned"), v)
            ser(STT(arot[:, :], M[4], 0.125, cosin[:, 1, :], ALU.mult, ALU.mult))
            ser(STT(aq[s_][:, :], aq[s_][:, :], 0.125, cosin[:, 0, :], ALU.mult, ALU.mult))
            ser.flag(TT(aq[s_][:, :], aq[s_][:, :], arot[:, :], ALU.add), "q_rotated", v)
            dve.wait_ge(ev("q_rest"), v)
            ser.flag(STT(T[2], q_, 0.0, T[2], ALU.min, ALU.subtract), "q_ls", v)
            dve.wait_ge(ev("f_sig"), v)
            ser(TS(kk[:, :], T[1], curh[s_][:, 2:3], curh[s_][:, 3:4], ALU.mult, ALU.subtract))
            dve.wait_ge(ev("lnf"), v)
            for n in range(NT):
                tk = slice(P * n, P * n + P)
                ins = V.tensor_tensor_scan(bb[:, tk], T[0][:, tk], lnc[:, :], 0.0, ALU.add, ALU.subtract)
                if n < 3:
                    ser(ins)
                else:
                    ser.flag(ins, "b_ready", v)
            dve.wait_ge(ev("q_sig"), v)
            ser.flag(TT(q_, q_, T[2], ALU.mult), "qk_ready", v)

            def mul(n):
                L = 64 >> n
                dve.wait_ge(ev("level_exp"), v * 7 - 7 + n + 1)
                if n >= 2:
                    dve.wait_ge(ev("item_done"), v * 8 - 8 + n)
                xv = lev[:, n % 3, :].rearrange("p (m w) -> p m w", w=2 * L)
                qv = q_.rearrange("p (m w) -> p m w", w=2 * L)
                kv = kk[:, :].rearrange("p (m w) -> p m w", w=2 * L)
                ser(TT(qt[:, n % 2, :].rearrange("p (m w) -> p m w", w=L), qv[:, :, L:2 * L], xv[:, :, L:2 * L], ALU.mult))
                ser.flag(TT(kt[:, n % 2, :].rearrange("p (m w) -> p m w", w=2 * L)[:, :, 0:L], kv[:, :, 0:L], xv[:, :, 0:L], ALU.mult),
                         "level_mul", v * 7 - 7 + n + 1)

            def use(n):
                L = 64 >> n
                dve.wait_ge(ev("item_done"), v * 8 - 8 + n + 2)
                V.memset(tick[:, 3:4], 0.0)
                ser.flag(V.copy_predicated(p_diag[:, :].rearrange("p (m w) -> p m w", w=2 * L)[:, :, L:2 * L],
                                           lmask[:, n, :].rearrange("p (m w) -> p m w", w=L),
                                           M[4 + (n + 1) % 2][:, 0:256].rearrange("p (m w) -> p m w", w=L)),
                         "item_used", v * 8 - 8 + n + 2)

            dve.wait_ge(ev("block_exp"), v)
            ser(TT(qe[:, :], qe[:, :], q_[:, P:S], ALU.mult))
            ser(TT(kg[:, :], kg[:, :], kk[:, 0:384], ALU.mult))
            ser(TS(xe[:, 0:256], qe[:, P:384], etot[:, 1:2], None, ALU.mult))
            ser(TS(xe[:, P:256], qe[:, 256:384], etot[:, 2:3], None, ALU.mult))
            ser.flag(TS(xe[:, 256:384], xe[:, P:256], etot[:, 1:2], None, ALU.mult), "block_mul", v)
            mul(0)
            mul(1)
            dve.wait_ge(ev("item_done"), v * 8 - 7)
            ser.flag(TT(p_diag[:, :].rearrange("p (n c) -> p n c", n=NT), M[4].rearrange("p (n c) -> p n c", n=NT),
                        ident.unsqueeze(1).broadcast_to([P, NT, P]), ALU.mult), "item_used", v * 8 - 7)
            dve.wait_ge(ev("scores_done"), v)
            sink = curh[s_][:, 4:6].unsqueeze(2).broadcast_to([P, 2, 4])
            sv = lambda i: sm[:, i, :].rearrange("p (h n) -> p h n", h=2)
            ser(V.tensor_reduce(sm[:, 0, :], ps[:, 2:6, :].rearrange("p b (n w) -> p (b n) w", w=256), AX.X, ALU.max))
            ser(TT(sv(0), sv(0), sink, ALU.max))
            ser(TS(sm[:, 1, :], sm[:, 0, :], -1.0, None, ALU.mult))
            ser.flag(TT(sv(3), sink, sv(0), ALU.subtract), "neg_max", v)
            use(0)
            mul(2)
            use(1)
            mul(3)
            dve.wait_ge(ev("att_exp"), v)
            ser(TT(sm[:, 2, :], sm[:, 2, :], sm[:, 4, :], ALU.add))
            ser(V.reciprocal(sm[:, 5, :], sm[:, 2, :]))
            for g in range(8):
                pv = prob[:, g // 4, 256 * (g % 4):256 * (g % 4) + 256]
                ins = TS(pv, pv, sm[:, 5, g:g + 1], None, ALU.mult)
                if g < 7:
                    ser(ins)
                else:
                    ser.flag(ins, "p_normed", v)
            use(2)
            mul(4)
            for n, g in enumerate((hz[s_], az[s_])):
                dve.wait_ge(ev("z2_rest"), v * 2 - 1 + n)
                ser.flag(STT(T[n], g[:, :], 0.0, T[n], ALU.min, ALU.subtract), "z2_ls", v * 2 - 1 + n)
            use(3)
            mul(5)
            use(4)
            mul(6)
            use(5)
            for n, g in enumerate((hz[s_], az[s_])):
                dve.wait_ge(ev("z2_sig"), v * 2 - 1 + n)
                ser(TT(g[:, :], g[:, :], T[n], ALU.mult))
            use(6)
            dve.wait_ge(ev("att_done"), v)
            ser(TT(y[:, bass.ds(att_tile(j, b), 1), :].rearrange("p a n -> p (a n)"),
                   M[2], az[s_][:, :], ALU.mult))
            dve.wait_ge(ev("o_rstd"), v)
            ser(STT(T[2], M[4], par[:, R_GHEAD + l:R_GHEAD + l + 1], T[2], ALU.mult, ALU.mult))
            ser.flag(TT(y[:, bass.ds(j * 2 + b - 1, 1), :].rearrange("p a n -> p (a n)"), T[2], hz[s_][:, :], ALU.mult), "mix2_done", v + 1)
            assert ser.n == 34, ser.n

        for l in range(2):
            norm(2 + l, R_GPRE + 8 * l)
            dve.wait_ge(ev("k_turned"), l + 1)
            ser.at(2 * l, ev("dve_k_step"))
            ser(TT(arot[:, :], M[4], cosin[:, 1, :], ALU.mult))
            ser(TT(T[1], T[1], cosin[:, 0, :], ALU.mult))
            ser.flag(TT(arot[:, :], arot[:, :], T[1], ALU.add), "k_rotated", l + 1)
            half2(l, 0, 0, True, False)
            dve.wait_ge(ev("k_spread"), 64 * (l + 1))
            with nc.vector.Fori(0, 3) as j:
                half2(l, j, 1, True, True)
                half2(l, j + 1, 0, True, True)
            half2(l, 3, 1, True, True)
            half2(l, 4, 0, False, True)
            for n in range(KT):
                dve.wait_ge(*((ev("bank_done"), 7 + 7 * l + n + 1) if n < 7 else (unit, u_two + per_layer * l + 66)))
                ser.flag(V.tensor_copy(y[:, n, :], ps[:, n, :]), "post_copy", 8 * l + n + 1)
            dve.wait_ge(ev("post_rstd"), l + 1)
            for n in range(KT):
                g = R_GPOST + 8 * l + n
                ser.flag(STT(y[:, n, :], y[:, n, :], par[:, g:g + 1], rstd[:, :], ALU.mult, ALU.mult), "post_scaled", 8 * l + n + 1)
                if n % 2 == 1:
                    ser.flag(TT(x[:, n, :], x[:, n, :], y[:, n, :], ALU.add), "x_added", 8 + 4 * l + n // 2 + 1)
        for m in range(8):
            dve.wait_ge(ev("out_t"), m + 1)
            n, half_ = m % 4, m // 4
            V.tensor_copy(xout[:, n, 512 * half_:512 * half_ + 512], M[m % 4]).then_inc(ev("out_rows"), 1)
            dve.wait_ge(ev("out_rows"), m + 1)

    ctx.close()


_INS = ["x", "norm_mix_g", "w_in", "b_if", "b_gate", "conv_w", "mlstm_norm_g", "sb_q_norm_g", "sb_k_norm_g", "w_out",
        "norm_mlp_g", "w_up", "w_down", "w_in_2", "w_out_2", "g_pre_2", "g_post_2", "lb_param_2", "g_head_2", "sinks_2"]


def kernel(**inputs):
    import concourse.bacc as _bacc
    from concourse.bass_utils import run_bass_kernel_spmd as _run

    nc = _bacc.Bacc("TRN2", target_bir_lowering=False, num_devices=1)
    arrays, aps = {}, {}
    for name in _INS + ["consts"]:
        a = constants() if name == "consts" else np.ascontiguousarray(inputs[name])
        arrays[f"in_{name}_dram"] = a
        aps[name] = nc.dram_tensor(f"in_{name}_dram", a.shape, mybir.dt.from_np(a.dtype), kind="ExternalInput").ap()
    out = nc.dram_tensor("out_0_dram", (1, S, DM), F32, kind="ExternalOutput").ap()
    build(nc, aps, out)
    r = _run(nc, [arrays], core_ids=[0])
    return r.results[0]["out_0_dram"]
```
